# Optimizing a Trainium2 kernel written in Bass

```python
import jax
import jax.numpy as jnp
from jax import lax
import numpy as np

D_MODEL = 1024
BATCH = 1
SEQ = 256
DEPTH = 2

GRID_W = 64
CTX_LEN = 256
QBLK = 128
ROPE_THETA = 10000.0
EPS = 1e-6
NEG = -1e30
DH = 64
N_BRANCH = 4
BR_WIDTH = 8 * DH
H_A = 8
Q_LORA = 256
KV_LORA = 128
NOPE_A = 64
ROPE_A = 32
V_A = 64
H_B = 8
KV_B = 2
WINDOW = 128
H_C = 8
KH_MAX = 8
KW = 16
H_D = 8
KV_D = 2
D_FF = 256 * (-(-8 * D_MODEL // (3 * 256)))
MOD_CHUNKS = 6

IN_SPLITS = (
    ('a_cq', Q_LORA), ('a_ckv', KV_LORA), ('a_kr', ROPE_A),
    ('b_q', H_B * DH), ('b_k', KV_B * DH), ('b_v', KV_B * DH),
    ('c_q', H_C * DH), ('c_k', H_C * DH), ('c_v', H_C * DH),
    ('d_q', H_D * DH), ('d_k', KV_D * DH), ('d_v', KV_D * DH),
    ('gate', N_BRANCH * D_MODEL),
)
IN_COLS = sum(w for _, w in IN_SPLITS)

kernel_name = 'hybrid_gated_mixer_dit'

def rmsnorm(x, g):
    xf = x.astype(jnp.float32)
    y = xf * lax.rsqrt(jnp.mean(xf * xf, axis=-1, keepdims=True) + EPS)
    return (y * g.astype(jnp.float32)).astype(x.dtype)

def split_cols(p):
    out = {}
    off = 0
    for name, w in IN_SPLITS:
        out[name] = p[..., off:off + w]
        off += w
    return out

def heads(t, h):
    return t.reshape(t.shape[0], t.shape[1], h, t.shape[-1] // h)

def rope_1d(x, pos):
    d = x.shape[-1]
    inv = ROPE_THETA ** (-jnp.arange(d // 2, dtype=jnp.float32) * 2.0 / d)
    ang = pos.astype(jnp.float32)[:, None] * inv[None, :]
    cos = jnp.cos(ang)[:, None, :]
    sin = jnp.sin(ang)[:, None, :]
    xf = x.astype(jnp.float32)
    x1, x2 = xf[..., :d // 2], xf[..., d // 2:]
    return jnp.concatenate([x1 * cos - x2 * sin, x2 * cos + x1 * sin], axis=-1).astype(x.dtype)

def axial_rope(x, rows_pos, cols_pos):
    h = x.shape[-1] // 2
    return jnp.concatenate([rope_1d(x[..., :h], rows_pos), rope_1d(x[..., h:], cols_pos)], axis=-1)

def attend_dense(q, k, v, scale, sink=None):
    B, Tq, Hkv, G, dk = q.shape
    nb = Tq // QBLK
    qb = jnp.moveaxis(q.reshape(B, nb, QBLK, Hkv, G, dk), 1, 0)

    def block(qi):
        s = jnp.einsum('bqhgd,bkhd->bhgqk', qi, k, preferred_element_type=jnp.float32) * scale
        if sink is not None:
            sk = jnp.broadcast_to(sink.astype(jnp.float32)[None, :, :, None, None], s.shape[:-1] + (1,))
            p = jax.nn.softmax(jnp.concatenate([s, sk], axis=-1), axis=-1)[..., :-1]
        else:
            p = jax.nn.softmax(s, axis=-1)
        return jnp.einsum('bhgqk,bkhd->bqhgd', p.astype(v.dtype), v)

    o = lax.map(block, qb)
    return jnp.moveaxis(o, 0, 1).reshape(B, Tq, Hkv * G * v.shape[-1])

def attend_window(q, k, v, ck, cv, sink, scale):
    B, T, Hkv, G, d = q.shape
    L = ck.shape[1]
    nb = T // QBLK
    pad = ((0, 0), (QBLK, QBLK), (0, 0), (0, 0))

    def band(t):
        tp = jnp.pad(t, pad).reshape(B, nb + 2, QBLK, Hkv, t.shape[-1])
        tb = jnp.concatenate([tp[:, :-2], tp[:, 1:-1], tp[:, 2:]], axis=2)
        return jnp.moveaxis(tb, 1, 0)

    kb, vb = band(k), band(v)
    qb = jnp.moveaxis(q.reshape(B, nb, QBLK, Hkv, G, d), 1, 0)
    qi = jnp.arange(QBLK)[:, None] + QBLK
    kj = jnp.arange(3 * QBLK)[None, :]
    near = jnp.abs(qi - kj) <= WINDOW
    nloc = 3 * QBLK

    def block(args):
        n, qn, kn, vn = args
        kabs = n * QBLK - QBLK + kj
        valid = near & (kabs >= 0) & (kabs < T)
        s_loc = jnp.einsum('bqhgd,bkhd->bhgqk', qn, kn, preferred_element_type=jnp.float32) * scale
        s_loc = jnp.where(valid, s_loc, NEG)
        s_ctx = jnp.einsum('bqhgd,bkhd->bhgqk', qn, ck, preferred_element_type=jnp.float32) * scale
        s_snk = jnp.broadcast_to(sink.astype(jnp.float32)[None, :, :, None, None], s_loc.shape[:-1] + (1,))
        p = jax.nn.softmax(jnp.concatenate([s_loc, s_ctx, s_snk], axis=-1), axis=-1)
        p_loc = p[..., :nloc].astype(v.dtype)
        p_ctx = p[..., nloc:nloc + L].astype(v.dtype)
        return jnp.einsum('bhgqk,bkhd->bqhgd', p_loc, vn) + jnp.einsum('bhgqk,bkhd->bqhgd', p_ctx, cv)

    o = lax.map(block, (jnp.arange(nb), qb, kb, vb))
    return jnp.moveaxis(o, 0, 1).reshape(B, T, Hkv * G * d)

def attend_neighbourhood(q, k, v, ck, cv, rpb, scale):
    B, T, H, d = q.shape
    rows = T // GRID_W
    kh = min(KH_MAX, rows)
    nk = kh * GRID_W
    kg = k.reshape(B, rows, GRID_W, H, d)
    vg = v.reshape(B, rows, GRID_W, H, d)
    qg = jnp.moveaxis(q.reshape(B, rows, GRID_W, H, d), 1, 0)
    qc = jnp.arange(GRID_W)
    c0 = jnp.clip(qc - KW // 2, 0, GRID_W - KW)
    kc = jnp.arange(nk) % GRID_W
    kr_off = jnp.arange(nk) // GRID_W
    col_ok = (kc[None, :] >= c0[:, None]) & (kc[None, :] < c0[:, None] + KW)
    dc_idx = jnp.clip(kc[None, :] - qc[:, None], -(KW - 1), KW - 1) + (KW - 1)
    L = ck.shape[1]

    def row(args):
        r, qr = args
        r0 = jnp.clip(r - kh // 2, 0, rows - kh)
        kr = lax.dynamic_slice_in_dim(kg, r0, kh, axis=1).reshape(B, nk, H, d)
        vr = lax.dynamic_slice_in_dim(vg, r0, kh, axis=1).reshape(B, nk, H, d)
        dr_idx = jnp.clip(r0 + kr_off - r, -(KH_MAX - 1), KH_MAX - 1) + (KH_MAX - 1)
        bias = rpb[:, dr_idx[None, :], dc_idx].astype(jnp.float32)
        s_loc = jnp.einsum('bqhd,bkhd->bhqk', qr, kr, preferred_element_type=jnp.float32) * scale + bias
        s_loc = jnp.where(col_ok, s_loc, NEG)
        s_ctx = jnp.einsum('bqhd,bkhd->bhqk', qr, ck, preferred_element_type=jnp.float32) * scale
        p = jax.nn.softmax(jnp.concatenate([s_loc, s_ctx], axis=-1), axis=-1)
        p_loc = p[..., :nk].astype(v.dtype)
        p_ctx = p[..., nk:nk + L].astype(v.dtype)
        return jnp.einsum('bhqk,bkhd->bqhd', p_loc, vr) + jnp.einsum('bhqk,bkhd->bqhd', p_ctx, cv)

    o = lax.map(row, (jnp.arange(rows), qg))
    return jnp.moveaxis(o, 0, 1).reshape(B, T, H * d)

def gated_merge(gate_pre, branches, w_branch, w_out):
    o = jnp.stack(branches, axis=2)
    up = jnp.einsum('btnw,nwd->btnd', o, w_branch)
    g = jax.nn.sigmoid(gate_pre.reshape(up.shape))
    return jnp.sum(g * up, axis=2) @ w_out

def swiglu(u, w1, w2):
    a, b = jnp.split(u @ w1, 2, axis=-1)
    return (jax.nn.silu(a) * b) @ w2

def token_mixers(ux, uc, rows_pos, cols_pos, ctx_out, w_in, g_a_q, g_a_kv, w_a_uq, w_a_ukv,
                 sink_b, rpb_c, g_d_q, g_d_k, w_branch, w_out):
    B, T, _ = ux.shape
    L = uc.shape[1]
    px = split_cols(ux @ w_in)
    pc = split_cols(uc @ w_in)
    rope = lambda t: axial_rope(t, rows_pos, cols_pos)
    g_b = H_B // KV_B
    g_d = H_D // KV_D
    s_a = (NOPE_A + ROPE_A) ** -0.5
    s_h = DH ** -0.5

    def mla_q(p):
        return heads(rmsnorm(p['a_cq'], g_a_q) @ w_a_uq, H_A)

    def mla_kv(p, rotate):
        kv = heads(rmsnorm(p['a_ckv'], g_a_kv) @ w_a_ukv, H_A)
        kr = p['a_kr'][:, :, None, :]
        if rotate:
            kr = rope(kr)
        k = jnp.concatenate([kv[..., :NOPE_A], jnp.broadcast_to(kr, kv.shape[:-1] + (ROPE_A,))], axis=-1)
        return k, kv[..., NOPE_A:]

    qa = mla_q(px)
    qa = jnp.concatenate([qa[..., :NOPE_A], rope(qa[..., NOPE_A:])], axis=-1)
    ka, va = mla_kv(px, True)
    kca, vca = mla_kv(pc, False)
    oa = attend_dense(qa[:, :, :, None], jnp.concatenate([ka, kca], axis=1),
                      jnp.concatenate([va, vca], axis=1), s_a)

    qb = rope(heads(px['b_q'], H_B)).reshape(B, T, KV_B, g_b, DH)
    kb = rope(heads(px['b_k'], KV_B))
    vb = heads(px['b_v'], KV_B)
    kcb = heads(pc['b_k'], KV_B)
    vcb = heads(pc['b_v'], KV_B)
    sink = sink_b.reshape(KV_B, g_b)
    ob = attend_window(qb, kb, vb, kcb, vcb, sink, s_h)

    kcc = heads(pc['c_k'], H_C)
    vcc = heads(pc['c_v'], H_C)
    oc = attend_neighbourhood(heads(px['c_q'], H_C), heads(px['c_k'], H_C), heads(px['c_v'], H_C),
                              kcc, vcc, rpb_c, s_h)

    qd = rope(rmsnorm(heads(px['d_q'], H_D), g_d_q)).reshape(B, T, KV_D, g_d, DH)
    kd = rope(rmsnorm(heads(px['d_k'], KV_D), g_d_k))
    vd = heads(px['d_v'], KV_D)
    kcd = rmsnorm(heads(pc['d_k'], KV_D), g_d_k)
    vcd = heads(pc['d_v'], KV_D)
    od = attend_dense(qd, jnp.concatenate([kd, kcd], axis=1), jnp.concatenate([vd, vcd], axis=1), s_h)

    yx = gated_merge(px['gate'], (oa, ob, oc, od), w_branch, w_out)
    if not ctx_out:
        return yx, None

    oca = attend_dense(mla_q(pc)[:, :, :, None], kca, vca, s_a)
    ocb = attend_dense(heads(pc['b_q'], H_B).reshape(B, L, KV_B, g_b, DH), kcb, vcb, s_h, sink)
    occ = attend_dense(heads(pc['c_q'], H_C)[:, :, :, None], kcc, vcc, s_h)
    ocd = attend_dense(rmsnorm(heads(pc['d_q'], H_D), g_d_q).reshape(B, L, KV_D, g_d, DH), kcd, vcd, s_h)
    yc = gated_merge(pc['gate'], (oca, ocb, occ, ocd), w_branch, w_out)
    return yx, yc

def setup_inputs(seed: int = 0) -> dict:
    key = jax.random.key(seed)
    ks = jax.random.split(key, 23)
    f32 = jnp.float32

    def nrm(k, shape, std):
        return jax.random.normal(k, shape, f32) * std

    def gain(k, n):
        return 1.0 + 0.05 * jax.random.normal(k, (DEPTH, n), f32)

    L = DEPTH
    return {
        'x': nrm(ks[0], (BATCH, SEQ, D_MODEL), 1.0),
        'c': nrm(ks[1], (BATCH, D_MODEL), 1.0),
        'ctx': nrm(ks[2], (BATCH, CTX_LEN, D_MODEL), 1.0),
        'c_ctx': nrm(ks[3], (D_MODEL,), 1.0),
        'w_mod': nrm(ks[4], (L, D_MODEL, MOD_CHUNKS * D_MODEL), 0.5 * D_MODEL ** -0.5),
        'b_mod': nrm(ks[5], (L, MOD_CHUNKS * D_MODEL), 0.02),
        'g_pre_mix': gain(ks[6], D_MODEL),
        'g_post_mix': gain(ks[7], D_MODEL),
        'g_pre_ffn': gain(ks[8], D_MODEL),
        'g_post_ffn': gain(ks[9], D_MODEL),
        'w_in': nrm(ks[10], (L, D_MODEL, IN_COLS), D_MODEL ** -0.5),
        'g_a_q': gain(ks[11], Q_LORA),
        'g_a_kv': gain(ks[12], KV_LORA),
        'w_a_uq': nrm(ks[13], (L, Q_LORA, H_A * (NOPE_A + ROPE_A)), Q_LORA ** -0.5),
        'w_a_ukv': nrm(ks[14], (L, KV_LORA, H_A * (NOPE_A + V_A)), KV_LORA ** -0.5),
        'sink_b': nrm(ks[15], (L, H_B), 0.5),
        'rpb_c': nrm(ks[16], (L, H_C, 2 * KH_MAX - 1, 2 * KW - 1), 0.2),
        'g_d_q': gain(ks[17], DH),
        'g_d_k': gain(ks[18], DH),
        'w_branch': nrm(ks[19], (L, N_BRANCH, BR_WIDTH, D_MODEL), BR_WIDTH ** -0.5),
        'w_out': nrm(ks[20], (L, D_MODEL, D_MODEL), D_MODEL ** -0.5),
        'w_ffn_in': nrm(ks[21], (L, D_MODEL, 2 * D_FF), D_MODEL ** -0.5),
        'w_ffn_out': nrm(ks[22], (L, D_FF, D_MODEL), D_FF ** -0.5),
    }

def reference(x, c, ctx, c_ctx, w_mod, b_mod, g_pre_mix, g_post_mix, g_pre_ffn, g_post_ffn,
              w_in, g_a_q, g_a_kv, w_a_uq, w_a_ukv, sink_b, rpb_c, g_d_q, g_d_k,
              w_branch, w_out, w_ffn_in, w_ffn_out):
    T = x.shape[1]
    t = jnp.arange(T)
    rows_pos = t // GRID_W
    cols_pos = t % GRID_W
    sc = jax.nn.silu(c)
    scc = jax.nn.silu(c_ctx)
    h, hc = x, ctx
    for l in range(DEPTH):
        last = l == DEPTH - 1
        sh1x, sc1x, ga1x, sh2x, sc2x, ga2x = jnp.split((sc @ w_mod[l] + b_mod[l])[:, None, :], MOD_CHUNKS, axis=-1)
        sh1c, sc1c, ga1c, sh2c, sc2c, ga2c = jnp.split(scc @ w_mod[l] + b_mod[l], MOD_CHUNKS, axis=-1)
        ux = rmsnorm(h, g_pre_mix[l]) * (1 + sc1x) + sh1x
        uc = rmsnorm(hc, g_pre_mix[l]) * (1 + sc1c) + sh1c
        yx, yc = token_mixers(ux, uc, rows_pos, cols_pos, not last, w_in[l], g_a_q[l], g_a_kv[l],
                              w_a_uq[l], w_a_ukv[l], sink_b[l], rpb_c[l], g_d_q[l], g_d_k[l],
                              w_branch[l], w_out[l])
        h = h + ga1x * rmsnorm(yx, g_post_mix[l])
        ux = rmsnorm(h, g_pre_ffn[l]) * (1 + sc2x) + sh2x
        h = h + ga2x * rmsnorm(swiglu(ux, w_ffn_in[l], w_ffn_out[l]), g_post_ffn[l])
        if not last:
            hc = hc + ga1c * rmsnorm(yc, g_post_mix[l])
            uc = rmsnorm(hc, g_pre_ffn[l]) * (1 + sc2c) + sh2c
            hc = hc + ga2c * rmsnorm(swiglu(uc, w_ffn_in[l], w_ffn_out[l]), g_post_ffn[l])
    return h


_drawn_inputs = setup_inputs


def setup_inputs(seed=0):
    import zlib

    import numpy as np

    out = dict(_drawn_inputs(seed))
    spreads = {}
    factors = {'g_pre_mix': 3.043,
     'g_post_ffn': 2.845,
     'g_a_q': 8.0,
     'g_a_kv': 4.893,
     'sink_b': 64.0,
     'rpb_c': 6.678,
     'g_d_q': 8.0,
     'g_d_k': 8.0}
    for name, (base, spread) in spreads.items():
        noise = np.random.default_rng([zlib.crc32(name.encode()), seed]).standard_normal(out[name].shape)
        drawn = base * np.exp(spread * noise) if base else spread * noise
        out[name] = jnp.asarray(drawn.astype(out[name].dtype))
    for name, factor in factors.items():
        out[name] = (out[name] * factor).astype(out[name].dtype)
    return out
```

```python
from contextlib import ExitStack

import numpy as np
import concourse.bass as bass
from concourse import mybir

ALU = mybir.AluOpType
ACT = mybir.ActivationFunctionType
F32 = mybir.dt.float32
F32R = mybir.dt.float32r
AX_X = mybir.AxisListType.X

P = 128
DEPTH, D, SEQ, CTX, DFF, DH = 2, 1024, 256, 256, 2816, 64
NTOK = SEQ + CTX
KT = D // P
GRID = 64
KWIN = 16
EPS = 1e-6
NEG = -1e30
QL, KVL, NOPE, ROPE = 256, 128, 64, 32
DA = NOPE + ROPE
WIDTHS = (('a_cq', QL), ('a_ckv', KVL), ('a_kr', ROPE), ('b_q', 512), ('b_k', 128), ('b_v', 128),
          ('c_q', 512), ('c_k', 512), ('c_v', 512), ('d_q', 512), ('d_k', 128), ('d_v', 128), ('gate', 4 * D))
OFF = {}
for _n, _w in WIDTHS:
    OFF[_n] = sum(w for _, w in WIDTHS[:len(OFF)])
FT = DFF // P
PIECE = 512
W_RING = 4
AHEAD = 3
ROWS = 85

CONST = {}
for _n, _w in (('ident', 128), ('rotB', 128), ('rotA', 128), ('cosB', 256), ('sinB', 256), ('cosA', 256),
               ('sinA', 256), ('maskB', 512), ('maskC', 64), ('halves', 2), ('ones', 1), ('power', 8)):
    CONST[_n] = (CONST[_p][1] if CONST else 0, (CONST[_p][1] if CONST else 0) + _w)
    _p = _n
NCONST = CONST['power'][1]

O_HI, O_LO, Q_AT, K_AT, V_AT, PT_AT = 0, 8192, 16384, 18432, 20480, 22528
ARENA = PT_AT + 4096
M_HI, M_LO = Q_AT, Q_AT + KT * NTOK
H_HI, H_LO = 0, FT * NTOK
CQ_HI, CQ_LO, CKV_HI, CKV_LO = O_HI + 6144, O_HI + 7168, O_LO + 6144, O_LO + 6656
BIAS_AT = (O_HI + 6144, O_LO + 6144)
RAW_AT, P_AT, PN_AT, BT_AT = 0, 1536, 2560, 3584
FARENA = 4096

RINGS = {'acc': 3, 'raw': 3, 'tmp': 2, 'fil': 2, 'Q': 2, 'K': 2, 'V': 2, 'S': 2, 'P': 2, 'Pn': 2, 'T': 2,
         'PT': 2, 'pv': 1, 'w': W_RING, 'load': W_RING, 'macc': 2, 'bias': 2, 'tab': 2, 'small': 2}

SIGNALS = {
    'xin': ('xin_turned', 'xin_done'), 'cin': ('c_sig', 'c_silu', 'c_turned', 'c_done'),
    'par': ('par_turned', 'par_done'), 'mm': ('piece_used',), 'split': ('w_hi', 'w_lo'),
    'modadd': ('mod_ready',), 'coef': ('coef_ready',),
    'sq': ('sq_done',), 'sqsum': ('sq_sum',), 'stat': ('stat_sum', 'stat_mean', 'stat_rstd', 'stat_wide'),
    'bcast': ('rstd_bcast',), 'apA': ('ap_scaled', 'ap_hi', 'ap_full'), 'apB': ('ap_lo',),
    'post': ('post_scaled',), 'posth': ('h_new',),
    'evac': ('raw_ready',), 'evacsq': ('rawsq_ready',), 'gn': ('normed',), 'rot': ('rotated',),
    'rope': ('rope_sin', 'rope_cos', 'roped'), 'qks': ('op_hi', 'op_lo'), 'vtr': ('v_turned',), 'vs': ('v_hi', 'v_lo'),
    'tab': (), 'bias': ('bias_full', 'bias_hi', 'bias_lo'),
    'sc': ('scores',), 'mx': ('max_ready', 'negmax_ready'), 'ex': ('exp_done',),
    'sinksum': ('sum_ready',), 'den': ('rec_ready', 'prob_ready'),
    'tr': ('p_turned',), 'trs': ('pt_hi', 'pt_lo'), 'pv': ('pv_done',), 'ov': ('o_hi', 'o_lo'),
    'gsig': ('gate_sig',), 'gmul': ('gate_mul',), 'gacc': ('gate_acc',), 'ms': ('m_hi', 'm_lo'),
    'yev': ('y_ready',), 'fsig': ('ffn_sig', 'ffn_silu'), 'fh': ('ffn_h', 'hid_hi', 'hid_lo'),
    'tout': ('out_turned', 'out_copied'),
}


class Plan:

    def __init__(self):
        self.steps, self.tile, self.item, self.group = [], {}, {}, {}
        self.slot, self.freed, self.users = {}, {}, {r: [] for r in RINGS}
        self.pieces, self.kgen, self.last_main, self.before = [], {}, None, {}

    def step(self, kind, key, **facts):
        self.steps.append((kind, key, facts))

    def take(self, ring, key, *frees):
        users = self.users[ring]
        n = RINGS[ring]
        self.slot[ring, key] = len(users) % n
        self.freed[ring, key] = users[-n] if len(users) >= n else ()
        users.append(frees)

    def gemm(self, key, pieces, src, kt_of, rows, n, frees, need=(), exact=False):
        self.take('acc', key, *frees)
        self.tile[key] = dict(pieces=pieces, src=src, kt=kt_of, rows=rows, n=n, need=need, exact=exact)
        out = []
        for j, _ in enumerate(pieces):
            out.append(('mm', (key, j), {}))
        return out


def win_pieces(l, name, c0, cols=P, halves=None):
    starts = [OFF[name] + h * DH for h in halves] if halves else [OFF[name] + c0]
    return [dict(w='w_in', l=l, row=4 * j, nk=4, cols=cols, starts=starts) for j in range(2)]


def build_plan():
    p = Plan()
    S = p.steps

    def norm_stat(nm, srcs, nh, dim, n, frees):
        p.take('acc', ('stat', nm), ('stat_mean', nm))
        p.step('stat', nm, srcs=srcs, nh=nh, dim=dim, n=n)
        p.take('acc', ('bc', nm), *frees)
        p.step('bcast', nm, n=n)

    def square(nm, kt, n, what, made):
        if kt:
            p.take('fil', ('sq', nm, kt), ('sq_sum', (nm, kt)))
        else:
            p.before[nm], p.last_main = p.last_main, nm
        p.step('sq', (nm, kt), n=n, what=what, made=made)
        if kt:
            p.step('sqsum', (nm, kt), n=n)

    def apply(nm, l, which, n):
        for kt in range(KT + 1):
            if kt < KT:
                p.take('tmp', ('ap', nm, kt), ('ap_hi', (nm, kt)), ('ap_full', (nm, kt)))
                p.take('fil', ('ap', nm, kt), ('ap_lo', (nm, kt)))
                p.step('apA', (nm, kt), l=l, which=which, n=n)
            if kt:
                p.step('apB', (nm, kt - 1), n=n)

    def post(nm, l, which, n, then):
        for kt in range(KT + 1):
            if kt < KT:
                p.take('tmp', ('post', nm, kt), ('h_new', (nm, kt)))
                p.step('post', (nm, kt), n=n)
            if kt:
                p.step('posth', (nm, kt - 1), l=l, which=which, n=n)
                if then:
                    square(then, kt - 1, n, 'H', ('h_new', (nm, kt - 1)))

    def mods(l, chunks):
        for ch in chunks:
            key = ('mod', l, ch)
            S.extend(p.gemm(key, [dict(w='w_mod', l=l, row=4 * j, nk=4, cols=P, starts=[ch * P]) for j in range(2)],
                            'sc', lambda j: range(4 * j, 4 * j + 4), P, 2, [('mod_ready', (l, ch))], exact=True))
            p.step('modadd', (l, ch))

    p.take('acc', ('cin',), ('c_done', 0))
    p.step('cin', 0)
    for l in range(DEPTH):
        p.take('acc', ('par', l), ('par_done', l))
        p.step('par', l)
    for kt in range(KT):
        p.take('acc', ('xin', kt), ('xin_done', kt))
        p.step('xin', kt)
        square((0, 'pre_mix'), kt, NTOK, 'H', ('xin_done', kt))
    mods(0, range(0, 16))
    p.step('coef', (0, 0))

    for l in range(DEPTH):
        last = l == DEPTH - 1
        nq = SEQ if last else NTOK
        nm = (l, 'pre_mix')
        norm_stat(nm, None, 1, D, NTOK, [('ap_scaled', (nm, KT - 1))])
        apply(nm, l, 0, NTOK)
        if l == 0:
            late_mods = list(range(16, 48))
        need_u = {0: [('ap_lo', (nm, 3))], 1: [('ap_lo', (nm, 7))]}

        def proj(name, key, n, c0=0, cols=P, halves=None, frees=(), need=None):
            return p.gemm(key, win_pieces(l, name, c0, cols, halves), 'U', lambda j: range(4 * j, 4 * j + 4), cols, n,
                          frees, need or {})

        ckv, kr, cq = (l, 'ckv'), (l, 'kr'), [(l, 'cq', 0), (l, 'cq', 1)]
        S.extend(proj('a_ckv', ckv, NTOK, frees=[('rawsq_ready', ckv)], need=need_u))
        p.take('raw', ckv, ('op_hi', ckv), ('op_lo', ckv))
        p.take('fil', ckv, ('stat_sum', ckv))
        p.step('evac', ckv, rows=(0, P), n=NTOK)
        p.step('evacsq', ckv, rows=(0, P), n=NTOK)
        for t, k in enumerate(cq):
            S.extend(proj('a_cq', k, nq, c0=t * P, frees=[('rawsq_ready', k)]))
            if t == 0:
                norm_stat(ckv, [ckv], 1, KVL, NTOK, [('normed', ckv)])
                p.step('gn', ckv, bc=ckv, n=NTOK, g=(l, 82))
                p.step('qks', ckv, src='raw', rows=(0, P), n=NTOK, dst=('ckv', 0))
            p.take('raw', k, ('op_hi', k), ('op_lo', k))
            p.take('fil', k, ('stat_sum', cq[1]))
            p.step('evac', k, rows=(0, P), n=nq)
            p.step('evacsq', k, rows=(0, P), n=nq)
        S.extend(proj('a_kr', kr, NTOK, c0=-NOPE, cols=DA, frees=[('raw_ready', kr)]))
        norm_stat(cq[1], cq, 1, QL, nq, [('normed', cq[1])])
        p.take('raw', kr, ('op_hi', kr), ('op_lo', kr))
        p.step('evac', kr, rows=(0, DA), n=NTOK)
        for t, k in enumerate(cq):
            p.step('gn', k, bc=cq[1], n=nq, g=(l, 80 + t))
            p.step('qks', k, src='raw', rows=(0, P), n=nq, dst=('cq', t))
        p.take('acc', ('rot', kr), ('rope_sin', kr))
        p.step('rot', kr, rows=DA, t='A', normed=False)
        p.take('tmp', ('rope', kr), ('roped', kr))
        p.step('rope', kr, rows=DA, t='A')
        p.step('qks', kr, src='raw', rows=(NOPE, DA), n=NTOK, dst=('kr', 0))

        units = [('A', h, [h]) for h in range(8)] + [('B', j, [j, j + 4]) for j in range(4)] \
            + [('C', j, [2 * j, 2 * j + 1]) for j in range(4)] + [('D', j, [j, j + 4]) for j in range(4)]
        kgen, items, of_unit = {}, [], []
        for b, j, heads in units:
            u = (l, b, j)
            kgen[u] = (l, b, 0) if b in 'BD' else u
            mine = []
            for h in heads:
                mine += [(u, h, 'x', 0), (u, h, 'x', 1)] + ([] if last else [(u, h, 'c', 0)])
            items += mine
            of_unit.append(mine)
        last_item = {}
        for it in items:
            last_item[it[0]] = it
            last_item['K', kgen[it[0]]] = it
        late = []

        def pieces_then(make):
            steps = []

            def first():
                steps.extend(make())
                S.append(steps.pop(0))
            return first, lambda: S.append(steps.pop(0))

        def chain(key, kind, n, make, ring, gen, free, rows=P, g=None):
            first, rest = pieces_then(make)
            out = [first] if kind == 'A' else [first, rest]

            def evac():
                p.take('raw', key, ('op_hi', key), ('op_lo', key))
                p.step('evac', key, rows=(0, rows), n=n)
                if kind == 'D':
                    p.take('fil', key, ('stat_sum', key))
                    p.step('evacsq', key, rows=(0, rows), n=n)

            def stat():
                p.take('acc', ('stat', key), ('stat_mean', key))
                p.step('stat', key, srcs=[key], nh=2, dim=DH, n=n)

            def gain():
                p.take('acc', ('bc', key), ('normed', key))
                p.step('bcast', key, n=n)
                p.step('gn', key, bc=key, n=n, g=g)

            def rotate():
                t = 'A' if kind == 'A' else 'B'
                p.take('acc', ('rot', key), ('rope_sin', key))
                p.step('rot', key, rows=rows, t=t, normed=kind == 'D')
                p.take('tmp', ('rope', key), ('roped', key))
                p.step('rope', key, rows=rows, t=t)

            def store():
                p.take(ring, gen, free)
                p.step('qks', key, src='acc' if kind == 'C' else 'raw', rows=(0, rows), n=n, dst=(ring, gen))
            if kind != 'C':
                out.append(evac)
            if kind == 'D':
                out += [stat, gain]
            if kind != 'C':
                out.append(rotate)
            return out + [store]

        def v_chain(key, gen, free, wide, make=None):
            out = []

            def evac():
                p.take('raw', key, ('v_turned', key))
                p.step('evac', key, rows=(P - wide, P), n=NTOK)

            def turn():
                p.take('acc', ('vtr', key), ('v_lo', key))
                p.step('vtr', key, wide=wide)

            def store():
                p.take('V', gen, free)
                p.step('vs', key, wide=wide, dst=gen)
            if make:
                out += list(pieces_then(make))
            return out + [evac, turn, store]

        def projection(u):
            _, b, j = u
            gen = kgen[u]
            qfree = ('scores', last_item[u])
            kfree = ('scores', last_item['K', gen])
            vfree = ('pv_done', last_item['K', gen][:3])
            if b == 'A':
                key, qkey = (l, 'A', 'kv', j), (l, 'A', 'q', j)

                def kv():
                    S.extend(p.gemm(key, [dict(w='ukv', l=l, h=j)], 'ckv', lambda _: range(1), P, NTOK,
                                    [('op_lo', key), ('raw_ready', key)], {0: [('op_lo', ckv)]}))

                def kstore():
                    p.take('K', gen, kfree)
                    p.step('qks', key, src='acc', rows=(0, NOPE), n=NTOK, dst=('K', gen))
                qs = chain(qkey, 'A', nq, lambda: p.gemm(
                    qkey, [dict(w='uq', l=l, h=j)], 'cq', lambda _: range(2), DA, nq, [('raw_ready', qkey)],
                    {0: [('op_lo', cq[1]), ('op_lo', cq[0])]}), 'Q', u, qfree, rows=DA)
                vs = v_chain(key, gen, vfree, DH)
                return [qs[0], kv, qs[1], vs[0], kstore, qs[2], vs[1], qs[3], vs[2]]
            low = b.lower()
            halves = [j, j + 4] if b in 'BD' else None
            own = j * P if b == 'C' else 0
            done = 'op_lo' if b == 'C' else 'rawsq_ready' if b == 'D' else 'raw_ready'
            qkey, nkey, vkey = ((l, b, x, j) for x in 'qkv')
            qs = chain(qkey, b, nq, lambda: proj(low + '_q', qkey, nq, c0=j * P, halves=halves,
                                                 frees=[(done, qkey)]), 'Q', u, qfree, g=(l, 83))
            if gen != u and j:
                return qs
            ks = chain(nkey, b, NTOK, lambda: proj(low + '_k', nkey, NTOK, c0=own, frees=[(done, nkey)]),
                       'K', gen, kfree, g=(l, 84))
            vs = v_chain(vkey, gen, vfree, P, lambda: proj(low + '_v', vkey, NTOK, c0=own,
                                                           frees=[('raw_ready', vkey)]))
            if b == 'C':
                return ks + qs + vs
            if b == 'B':
                return ks[:3] + qs[:2] + [ks[3], qs[2]] + vs[:3] + [qs[3], ks[4], vs[3], qs[4], vs[4]]
            return ks[:3] + qs[:2] + [ks[3], qs[2], ks[4], vs[0], vs[1], ks[5], vs[2], qs[3], ks[6], qs[4], vs[3], qs[5],
                                      vs[4], qs[6]]

        def bias_steps(u):
            p.take('bias', u, ('scores', last_item[u]))
            for i in range(2):
                p.take('tab', (u, i), ('bias_full', (u, i)))
                p.step('tab', (u, i))
                p.step('bias', (u, i), l=l)

        def emit(item_no):
            k = item_no
            if k < len(items):
                it = items[k]
                p.take('S', it, ('exp_done', it))
                p.take('P', it, ('prob_ready', it))
                p.take('Pn', it, ('p_turned', it))
                p.take('small', it, ('prob_ready', it))
                p.step('sc', it)
                p.step('mx', it)
            if 1 <= k <= len(items):
                if items[k - 1][0][1] == 'B':
                    p.step('sinksum', items[k - 1])
                p.step('den', items[k - 1])
            if k < len(items):
                p.step('ex', it)
            if 2 <= k < len(items) + 2:
                it2 = items[k - 2]
                g = it2[:3]
                ends = it2[2] == 'c' or it2[3] == 1
                if it2[3] == 0:
                    p.take('PT', g, ('pv_done', g))
                p.take('T', it2, ('pt_lo', it2))
                p.step('tr', it2)
                p.step('trs', it2)
            if 3 <= k < len(items) + 3:
                it3 = items[k - 3]
                if it3[2] == 'c' or it3[3] == 1:
                    g = it3[:3]
                    p.take('pv', g, ('o_lo', g))
                    p.step('pv', g)
                    p.step('ov', g)

        p.kgen.update(kgen)
        for micro in projection((l, 'A', 0)):
            micro()
        at_item = 0
        for un, mine in enumerate(of_unit):
            micro = []
            if un + 1 < len(units):
                u2 = (l, *units[un + 1][:2])
                micro = projection(u2)
                if u2[1] == 'C':
                    bias_steps(u2)
            put = 0
            for i in range(len(mine)):
                emit(at_item + i)
                upto = -(-len(micro) * (i + 1) // len(mine))
                for m in micro[put:upto]:
                    m()
                put = upto
            at_item += len(mine)
            if l == 0 and late_mods:
                mods(0, late_mods[:4])
                late_mods = late_mods[4:]
        for i in range(3):
            emit(at_item + i)
        if l == 0:
            if late_mods:
                mods(0, late_mods)
            p.step('coef', (0, 1))
            p.step('coef', (0, 2))

        for dt in range(KT):
            for n in range(4):
                k = (l, dt, n)
                S.extend(p.gemm(('gate', k), [dict(w='w_in', l=l, row=4 * j, nk=4, cols=P,
                                                   starts=[OFF['gate'] + n * D + dt * P]) for j in range(2)],
                                'U', lambda j: range(4 * j, 4 * j + 4), P, nq, [('gate_sig', k)]))
                p.take('tmp', ('gate', k), ('gate_mul', k))
                p.step('gsig', k, n=nq)
                S.extend(p.gemm(('up', k), [dict(w='w_branch', l=l, b=n, row=0, nk=4, cols=P, starts=[dt * P])],
                                'O', lambda _, n=n: range(4 * n, 4 * n + 4), P, nq, [('gate_mul', k)],
                                {0: [('o_lo', items[-1][:3])]}))
                if n == 0:
                    p.take('macc', (l, dt), ('m_lo', (l, dt)))
                else:
                    p.take('fil', ('gate', k), ('gate_acc', k))
                p.step('gmul', k, n=nq)
                if n:
                    p.step('gacc', k, n=nq)
            p.step('ms', (l, dt), n=nq)

        mod_next = iter(range(48)) if not last else iter(())

        def some_mods(count):
            ch = [c for _, c in zip(range(count), mod_next)]
            mods(l + 1, ch)

        def output(name, nmo, pieces_of, src, kts, need):
            for dt in range(KT):
                key = (nmo, dt)
                S.extend(p.gemm(('y', key), pieces_of(dt), src, kts, P, nq, [('sq_done', key)],
                                need if dt == 0 else {}))
                p.step('yev', key, n=nq)
                square(nmo, dt, nq, 'Y', ('piece_used', (('y', key), len(p.tile['y', key]['pieces']) - 1)))

        nmo = (l, 'post_mix')
        output('w_out', nmo, lambda dt: [dict(w='w_out', l=l, row=4 * j, nk=4, cols=P, starts=[dt * P])
                                         for j in range(2)], 'M', lambda j: range(4 * j, 4 * j + 4),
               {j: [('m_lo', (l, 4 * j + 3))] for j in range(2)})
        norm_stat(nmo, None, 1, D, nq, [('post_scaled', (nmo, KT - 1))])
        some_mods(2)
        nm2 = (l, 'pre_ffn')
        post(nmo, l, 0, nq, nm2)
        norm_stat(nm2, None, 1, D, nq, [('ap_scaled', (nm2, KT - 1))])
        some_mods(2)
        apply(nm2, l, 1, nq)
        for f in range(FT):
            need = {0: [('ap_lo', (nm2, 3))], 1: [('ap_lo', (nm2, 7))]} if f == 0 else {}
            k = (l, f)
            S.extend(p.gemm(('fa', k), [dict(w='w_ffn_in', l=l, row=4 * j, nk=4, cols=P, starts=[f * P])
                                        for j in range(2)], 'U', lambda j: range(4 * j, 4 * j + 4), P, nq,
                            [('ffn_silu', k)], need))
            p.take('tmp', ('ffn', k), ('ffn_h', k))
            p.step('fsig', k, n=nq)
            S.extend(p.gemm(('fb', k), [dict(w='w_ffn_in', l=l, row=4 * j, nk=4, cols=P, starts=[DFF + f * P])
                                        for j in range(2)], 'U', lambda j: range(4 * j, 4 * j + 4), P, nq,
                            [('ffn_h', k)]))
            p.take('fil', ('ffn', k), ('hid_lo', k))
            p.step('fh', k, n=nq)
            some_mods(2)
        nmf = (l, 'post_ffn')
        output('w_ffn_out', nmf,
               lambda dt: [dict(w='w_ffn_out', l=l, row=4 * j, nk=min(4, FT - 4 * j), cols=P, starts=[dt * P])
                           for j in range(-(-FT // 4))],
               'hid', lambda j: range(4 * j, min(4 * j + 4, FT)),
               {j: [('hid_lo', (l, min(4 * j + 3, FT - 1)))] for j in range(-(-FT // 4))})
        norm_stat(nmf, None, 1, D, nq, [('post_scaled', (nmf, KT - 1))])
        if not last:
            for g in range(3):
                p.step('coef', (l + 1, g))
        post(nmf, l, 1, nq, (l + 1, 'pre_mix') if not last else None)
    for tt in range(SEQ // P):
        for half in range(2):
            p.take('acc', ('tout', tt, half), ('out_copied', (tt, half)))
            p.step('tout', (tt, half))

    use = []
    for n, (kind, key, _) in enumerate(S):
        if kind == 'mm':
            t = p.tile[key[0]]
            use.append((n, key, t['exact']))
    p.pieces = [(key, p.tile[key[0]]['pieces'][key[1]], exact) for _, key, exact in use]
    for i, (_, key, exact) in enumerate(use):
        p.take('load', key, ('piece_used', key) if exact else ('w_lo', key))
    for _, key, exact in use:
        if not exact:
            p.take('w', key, ('piece_used', key))
    order, done, seen = [], 0, 0
    for st in S:
        if st[0] == 'mm':
            seen += 1
            while done < min(len(use), seen + AHEAD):
                if not use[done][2]:
                    order.append(('split', use[done][1], {}))
                done += 1
        order.append(st)
    p.steps = order
    return p




def build(nc, x, c, ctx, c_ctx, w_mod, b_mod, g_pre_mix, g_post_mix, g_pre_ffn, g_post_ffn, w_in, g_a_q, g_a_kv,
          w_a_uq, w_a_ukv, sink_b, bias_rows, g_d_q, g_d_k, w_branch, w_out, w_ffn_in, w_ffn_out, consts, out):
    plan = build_plan()
    steps, tile = plan.steps, plan.tile
    weights = dict(w_in=w_in, w_mod=w_mod, w_branch=w_branch, w_out=w_out, w_ffn_in=w_ffn_in, w_ffn_out=w_ffn_out)

    count, total = {}, {}
    for kind, key, _ in steps:
        for name in SIGNALS[kind]:
            total[name] = total.get(name, 0) + 1
            count[name, key] = total[name]
    landed, at_slot = {}, [0] * W_RING
    for key, pc, _ in plan.pieces:
        k = plan.slot['load', key]
        at_slot[k] += 16 * (len(pc['starts']) if 'starts' in pc else 1)
        landed[key] = (k, at_slot[k])

    with ExitStack() as es:
        def sb(name, shape, dt=F32):
            return es.enter_context(nc.sbuf_tensor(name, shape, dt))

        sem = {name: es.enter_context(nc.semaphore(name)) for name in total}
        load_sem = [es.enter_context(nc.semaphore(f"load{k}")) for k in range(W_RING)]
        s_const = es.enter_context(nc.semaphore("s_const"))
        s_rows = es.enter_context(nc.semaphore("s_rows"))
        s_x = es.enter_context(nc.semaphore("s_x"))
        s_init = es.enter_context(nc.semaphore("s_init"))
        s_tab = [es.enter_context(nc.semaphore(f"s_tab{k}")) for k in range(2)]
        s_out = es.enter_context(nc.semaphore("s_out"))

        H = sb("H", [P, KT, NTOK])
        U = [sb(f"U{a}", [P, KT, NTOK], F32R) for a in ('hi', 'lo')]
        Z = sb("Z", [P, ARENA], F32R)
        Y = sb("Y", [P, FARENA])
        load_ring = sb("load_ring", [P, W_RING, PIECE])
        w_ring = sb("w_ring", [P, W_RING, 2, PIECE], F32R)
        tmp = sb("tmp", [P, 2, NTOK])
        fil = sb("fil", [P, 2, NTOK])
        sqacc = sb("sqacc", [P, NTOK])
        wide = sb("wide", [P, NTOK])
        tab = sb("tab", [P, 2, 384])
        C = sb("C", [P, NCONST])
        ident_r = sb("ident_r", [P, P], F32R)
        mask_r = sb("mask_r", [P, 512], F32R)
        flat = tab[:, :, :].rearrange("p a b -> p (a b)")
        rows = flat[:, 0:DEPTH * P].rearrange("p (l c) -> p l c", l=DEPTH)
        crows = flat[0:16, DEPTH * P:(DEPTH + 3) * P].rearrange("p (l c) -> p l c", l=3)
        par = sb("par", [P, DEPTH, ROWS])
        sc = sb("sc", [P, 2, KT])
        mod = sb("mod", [P, DEPTH, 48, 2])
        coef = sb("coef", [P, DEPTH, 4, KT, 2])
        sink = sb("sink", [P, DEPTH, 8])
        sink8 = sb("sink8", [P, DEPTH, 8])
        stat = sb("stat", [P, 3, 8])
        small = sb("small", [P, 2, 12])
        bank = [es.enter_context(nc.psum_tensor(f"bank{i}", [P, 512], F32)) for i in range(8)]

        def const(name, rows_=P):
            return C[0:rows_, CONST[name][0]:CONST[name][1]]

        ident = const('ident')

        def acc(key):
            return bank[plan.slot['acc', key]]

        def s_bank(it):
            return bank[3 + plan.slot['S', it]]

        def t_bank(it):
            return bank[5 + plan.slot['T', it]]

        pv_bank = bank[7]

        def raw(key):
            at = RAW_AT + plan.slot['raw', key] * NTOK
            return Y[:, at:at + NTOK]

        def macc(key):
            at = plan.slot['macc', key] * NTOK
            return Y[:, at:at + NTOK]

        def y_tile(kt):
            return Y[:, kt * NTOK:(kt + 1) * NTOK]

        def prob(ring, it):
            at = (P_AT if ring == 'P' else PN_AT) + plan.slot[ring, it] * NTOK
            return Y[:, at:at + NTOK]

        def z(at, n=NTOK):
            return Z[:, at:at + n]

        def o_tile(part, i):
            return z((O_HI, O_LO)[part] + i * NTOK)

        def staged(ring, gen, part):
            at = {'Q': Q_AT, 'K': K_AT, 'V': V_AT}[ring] + (2 * plan.slot[ring, gen] + part) * NTOK
            return z(at)

        def pt(g, part):
            return z(PT_AT + (2 * plan.slot['PT', g] + part) * 1024, 1024).rearrange("p (k q) -> p k q", k=4)

        def bias_r(u, i, part):
            at = BIAS_AT[plan.slot['bias', u]] + (2 * i + part) * 384
            return z(at, 384)

        def operand(src, part, kt, n):
            if src == 'U':
                return U[part][:, kt, 0:n]
            at = {'cq': (CQ_HI, CQ_LO), 'ckv': (CKV_HI, CKV_LO), 'O': (O_HI, O_LO), 'M': (M_HI, M_LO),
                  'hid': (H_HI, H_LO)}[src][part] + kt * NTOK
            return z(at, n)

        def w_slice(key, part, kt):
            pc = tile[key[0]]['pieces'][key[1]]
            if part is None:
                s = load_ring[:, plan.slot['load', key], :]
            else:
                s = w_ring[:, plan.slot['w', key], part, :]
            cols = {'uq': DA, 'ukv': P}.get(pc['w'], pc.get('cols'))
            return s[:, kt * cols:(kt + 1) * cols]

        def piece_size(pc):
            return {'uq': 2 * DA, 'ukv': P}.get(pc['w']) or pc['nk'] * pc['cols']

        def last_piece(key):
            return key, len(tile[key]['pieces']) - 1

        def scale_of(it):
            return (DA if it[0][1] == 'A' else DH) ** -0.5

        def subs(it):
            return [(0, NTOK)] if it[2] == 'x' else [(0, CTX), (CTX, 2 * CTX)]

        def is_ab(l, which):
            return coef[:, l, which]

        def shift(l, which, kt, side):
            return mod[:, l, 24 * which + kt, side:side + 1]

        def split_places(eng, key, f):
            r0, r1 = f['rows']
            n = f['n']
            ring, gen = f['dst']
            if f['src'] == 'acc':
                eng.wait_ge(sem['piece_used'], count['piece_used', last_piece(key)])
                src = acc(key)[r0:r1, 0:n]
            else:
                ready = 'roped' if ('roped', key) in count else 'normed'
                eng.wait_ge(sem[ready], count[ready, key])
                src = raw(key)[r0:r1, 0:n]
            if ring in 'QK':
                for name, k_ in plan.freed[ring, gen]:
                    eng.wait_ge(sem[name], count[name, k_])
                return [(staged(ring, gen, 0)[r0:r1, 0:n], staged(ring, gen, 1)[r0:r1, 0:n], src)]
            if ring == 'kr':
                return [(z(K_AT + 2 * k * NTOK)[r0:r1, :], z(K_AT + (2 * k + 1) * NTOK)[r0:r1, :], src)
                        for k in range(2)]
            return [(operand(ring, 0, gen, n), operand(ring, 1, gen, n), src)]

        def v_places(key, f, part):
            w = f['wide']
            dst = staged('V', f['dst'], part).rearrange("p (t w) -> p t w", t=4)[:, :, 0:w]
            return dst, acc(('vtr', key))[:, 0:4 * w].rearrange("p (t w) -> p t w", t=4)

        def pt_places(it, part):
            if it[2] == 'x':
                q0 = it[3] * P
                return pt(it[:3], part)[:, :, q0:q0 + P], t_bank(it)[:, :].rearrange("p (k q) -> p k q", k=4)
            dst = pt(it[:3], part)[:, 0:2, :].rearrange("p k (t q) -> p k t q", t=2)
            return dst, t_bank(it)[:, :].rearrange("p (t k q) -> p k t q", t=2, k=2)

        def v_column(u, h):
            return {'A': 0, 'B': h // 4 * DH, 'C': h % 2 * DH, 'D': h // 4 * DH}[u[1]]

        def o_places(g):
            u, h, side = g
            i = 'ABCD'.index(u[1]) * 4 + h // 2
            r0 = h % 2 * DH
            t0 = 0 if side == 'x' else SEQ
            return (o_tile(0, i)[r0:r0 + DH, t0:t0 + SEQ], pv_bank[0:DH, 0:SEQ], o_tile(1, i)[r0:r0 + DH, t0:t0 + SEQ])

        block = es.enter_context(nc.Block())

        @block.sync
        def _(sp):
            sp.dma_start(crows[0:8, 0, :], c.rearrange("b (k p) -> (b k) p", p=P)).then_inc(s_rows, 16)
            sp.dma_start(crows[8:16, 0, :], c_ctx.rearrange("(k p) -> k p", p=P)).then_inc(s_rows, 16)
            sp.dma_start(C[:, :], consts).then_inc(s_const, 16)
            sp.dma_start(Y[:, 0:2048].rearrange("p (t d) -> p t d", t=2),
                         x.rearrange("b (t p) d -> p (b t) d", p=P)).then_inc(s_x, 16)
            sp.dma_start(Y[:, 2048:4096].rearrange("p (t d) -> p t d", t=2),
                         ctx.rearrange("b (t p) d -> p (b t) d", p=P)).then_inc(s_x, 16)
            for l in range(DEPTH):
                sp.dma_start(rows[0:48, l, :], b_mod[l].rearrange("(k p) -> k p", p=P)).then_inc(s_rows, 16)
                for i, g in enumerate((g_pre_mix, g_post_mix, g_pre_ffn, g_post_ffn)):
                    sp.dma_start(rows[48 + 8 * i:56 + 8 * i, l, :],
                                 g[l].rearrange("(k p) -> k p", p=P)).then_inc(s_rows, 16)
                sp.dma_start(rows[80:82, l, :], g_a_q[l].rearrange("(k p) -> k p", p=P)).then_inc(s_rows, 16)
                sp.dma_start(rows[82:83, l, :], g_a_kv[l:l + 1, :]).then_inc(s_rows, 16)
                for i, g in enumerate((g_d_q, g_d_k)):
                    for half in range(2):
                        sp.dma_start(rows[83 + i:84 + i, l, half * DH:(half + 1) * DH],
                                     g[l:l + 1, :]).then_inc(s_rows, 16)
                sp.dma_start(sink[:, l, :], sink_b[l:l + 1, :].to_broadcast([P, 8])).then_inc(s_rows, 16)
            for key, pc, _ in plan.pieces:
                for name, k_ in plan.freed['load', key]:
                    sp.wait_ge(sem[name], count[name, k_])
                dst = load_ring[:, plan.slot['load', key], 0:piece_size(pc)]
                done = load_sem[plan.slot['load', key]]
                l = pc['l']
                if pc['w'] == 'uq':
                    h = pc['h']
                    sp.dma_start(dst.rearrange("p (k m) -> p k m", k=2),
                                 w_a_uq[l, :, h * DA:(h + 1) * DA].rearrange("(k p) m -> p k m", p=P)).then_inc(done, 16)
                elif pc['w'] == 'ukv':
                    h = pc['h']
                    sp.dma_start(dst, w_a_ukv[l, :, h * P:(h + 1) * P]).then_inc(done, 16)
                else:
                    w = weights[pc['w']][l, pc['b']] if 'b' in pc else weights[pc['w']][l]
                    m = pc['cols'] // len(pc['starts'])
                    r0 = pc['row'] * P
                    for i, c0 in enumerate(pc['starts']):
                        sp.dma_start(dst.rearrange("p (k m) -> p k m", k=pc['nk'])[:, :, i * m:(i + 1) * m],
                                     w[r0:r0 + pc['nk'] * P, c0:c0 + m].rearrange("(k p) m -> p k m", p=P))\
                            .then_inc(done, 16)
            for tt in range(SEQ // P):
                sp.wait_ge(sem['out_copied'], count['out_copied', (tt, 1)])
                sp.dma_start(out[0, tt * P:(tt + 1) * P, :], Y[:, tt * D:(tt + 1) * D]).then_inc(s_out, 16)
            sp.wait_ge(s_out, 16 * (SEQ // P))

        n_rows = 16 * (2 + DEPTH * 12)

        @block.gpsimd
        def _(pool):
            for kind, key, f in steps:
                if kind == 'sqsum':
                    nm, kt = key
                    pool.wait_ge(sem['sq_done'], count['sq_done', key])
                    pool.wait_ge(sem['sq_done'], count['sq_done', (nm, 0)]) if kt == 1 else pool.wait_ge(sem['sq_sum'], count['sq_sum', (nm, kt - 1)])
                    n = f['n']
                    pool.tensor_tensor(sqacc[:, 0:n], sqacc[:, 0:n], fil[:, plan.slot['fil', ('sq', nm, kt)], 0:n],
                                       ALU.add).then_inc(sem['sq_sum'], 1)
                elif kind == 'stat':
                    m = f['n'] // P * f['nh']
                    pool.wait_ge(sem['stat_mean'], count['stat_mean', key])
                    if count['stat_rstd', key] > 1:
                        pool.wait_ge(sem['stat_wide'], count['stat_wide', key] - 1)
                    if count['stat_rstd', key] == 1:
                        pool.wait_ge(s_const, 16)
                    pool.tensor_tensor(stat[:, 1, 0:m], stat[:, 0, 0:m], const('power')[:, 0:m],
                                       ALU.pow).then_inc(sem['stat_rstd'], 1)
                elif kind == 'apA':
                    nm, kt = key
                    k2 = ('ap', nm, kt)
                    pool.wait_ge(sem['ap_scaled'], count['ap_scaled', key])
                    for name, k_ in plan.freed['fil', k2]:
                        pool.wait_ge(sem[name], count[name, k_])
                    pool.wait_ge(sem['coef_ready'], count['coef_ready', (f['l'], 2 * f['which'])])
                    for side in range(f['n'] // SEQ):
                        r = slice(side * SEQ, (side + 1) * SEQ)
                        ins = pool.tensor_scalar(fil[:, plan.slot['fil', k2], r], tmp[:, plan.slot['tmp', k2], r],
                                                 is_ab(f['l'], 2 * f['which'])[:, kt, side:side + 1],
                                                 shift(f['l'], f['which'], kt, side), ALU.mult, ALU.add)
                    ins.then_inc(sem['ap_full'], 1)
                elif kind == 'rope':
                    r = f['rows']
                    pool.wait_ge(sem['rotated'], count['rotated', key])
                    pool.tensor_tensor(raw(key)[0:r, 0:SEQ], raw(key)[0:r, 0:SEQ], const('cos' + f['t'], r),
                                       ALU.mult).then_inc(sem['rope_cos'], 1)
                elif kind == 'bias':
                    u, i = key
                    pool.wait_ge(sem['bias_full'], count['bias_full', key])
                    pool.wait_ge(sem['bias_hi'], count['bias_hi', key])
                    pool.tensor_tensor(bias_r(u, i, 1), Y[:, BT_AT:BT_AT + 384], bias_r(u, i, 0).bitcast(F32),
                                       ALU.subtract).then_inc(sem['bias_lo'], 1)
                elif kind == 'den':
                    pool.wait_ge(sem['rec_ready'], count['rec_ready', key])
                    for name, k_ in plan.freed['Pn', key]:
                        pool.wait_ge(sem[name], count[name, k_])
                    sm = small[:, plan.slot['small', key]]
                    for i, (a, b) in enumerate(subs(key)):
                        ins = pool.tensor_scalar(prob('Pn', key)[:, a:b], prob('P', key)[:, a:b], sm[:, 10 + i:11 + i],
                                                 None, ALU.mult)
                    ins.then_inc(sem['prob_ready'], 1)
                elif kind == 'gacc':
                    l, dt, n = key
                    pool.wait_ge(sem['gate_mul'], count['gate_mul', key])
                    pool.wait_ge(sem['gate_mul'], count['gate_mul', (l, dt, 0)]) if n == 1 else pool.wait_ge(sem['gate_acc'], count['gate_acc', (l, dt, n - 1)])
                    a = macc((l, dt))[:, 0:f['n']]
                    pool.tensor_tensor(a, a, fil[:, plan.slot['fil', ('gate', key)], 0:f['n']],
                                       ALU.add).then_inc(sem['gate_acc'], 1)
                elif kind == 'fh':
                    n = f['n']
                    pool.wait_ge(sem['ffn_h'], count['ffn_h', key])
                    pool.wait_ge(sem['hid_hi'], count['hid_hi', key])
                    pool.tensor_tensor(operand('hid', 1, key[1], n), fil[:, plan.slot['fil', ('ffn', key)], 0:n],
                                       operand('hid', 0, key[1], n).bitcast(F32),
                                       ALU.subtract).then_inc(sem['hid_lo'], 1)

        @block.scalar
        def _(act):
            act.wait_ge(s_const, 16)
            act.activation(ident_r[:, :], ident, ACT.Copy).then_inc(s_init, 1)
            act.activation(mask_r[:, :], const('maskB'), ACT.Copy).then_inc(s_init, 1)
            for kind, key, f in steps:
                if kind == 'cin':
                    act.wait_ge(s_rows, n_rows)
                    act.activation(crows[:, 1, :], crows[:, 0, :], ACT.Sigmoid).then_inc(sem['c_sig'], 1)
                elif kind == 'xin':
                    act.wait_ge(sem['xin_turned'], count['xin_turned', key])
                    act.activation(H[:, key, :], acc(('xin', key))[:, :], ACT.Copy).then_inc(sem['xin_done'], 1)
                elif kind == 'split':
                    sz = piece_size(tile[key[0]]['pieces'][key[1]])
                    act.wait_ge(load_sem[landed[key][0]], landed[key][1])
                    for name, k_ in plan.freed['w', key]:
                        act.wait_ge(sem[name], count[name, k_])
                    act.activation(w_ring[:, plan.slot['w', key], 0, 0:sz], load_ring[:, plan.slot['load', key], 0:sz],
                                   ACT.Copy).then_inc(sem['w_hi'], 1)
                elif kind == 'sq':
                    nm, kt = key
                    n = f['n']
                    act.wait_ge(sem[f['made'][0]], count[f['made']])
                    if kt:
                        for name, k_ in plan.freed['fil', ('sq', nm, kt)]:
                            act.wait_ge(sem[name], count[name, k_])
                        dst = fil[:, plan.slot['fil', ('sq', nm, kt)], 0:n]
                    else:
                        if plan.before[nm]:
                            act.wait_ge(sem['stat_sum'], count['stat_sum', plan.before[nm]])
                        dst = sqacc[:, 0:n]
                    src = H[:, kt, 0:n] if f['what'] == 'H' else acc(('y', key))[:, 0:n]
                    act.activation(dst, src, ACT.Square).then_inc(sem['sq_done'], 1)
                elif kind == 'yev':
                    act.wait_ge(sem['piece_used'], count['piece_used', last_piece(('y', key))])
                    act.activation(y_tile(key[1])[:, 0:f['n']], acc(('y', key))[:, 0:f['n']],
                                   ACT.Copy).then_inc(sem['y_ready'], 1)
                elif kind == 'apA':
                    nm, kt = key
                    k2 = ('ap', nm, kt)
                    act.wait_ge(sem['ap_scaled'], count['ap_scaled', key])
                    act.wait_ge(sem['coef_ready'], count['coef_ready', (f['l'], 2 * f['which'])])
                    for side in range(f['n'] // SEQ):
                        r = slice(side * SEQ, (side + 1) * SEQ)
                        ins = act.activation(U[0][:, kt, r], tmp[:, plan.slot['tmp', k2], r], ACT.Identity,
                                             bias=shift(f['l'], f['which'], kt, side),
                                             scale=is_ab(f['l'], 2 * f['which'])[:, kt, side:side + 1])
                    ins.then_inc(sem['ap_hi'], 1)
                elif kind in ('evac', 'evacsq'):
                    r0, r1 = f['rows']
                    n = f['n']
                    act.wait_ge(sem['piece_used'], count['piece_used', last_piece(key)])
                    src = acc(key)[r0:r1, 0:n]
                    if kind == 'evac':
                        for name, k_ in plan.freed['raw', key]:
                            act.wait_ge(sem[name], count[name, k_])
                        act.activation(raw(key)[r0:r1, 0:n], src, ACT.Copy).then_inc(sem['raw_ready'], 1)
                    else:
                        for name, k_ in plan.freed['fil', key]:
                            act.wait_ge(sem[name], count[name, k_])
                        act.activation(fil[r0:r1, plan.slot['fil', key], 0:n], src,
                                       ACT.Square).then_inc(sem['rawsq_ready'], 1)
                elif kind == 'qks':
                    for d in split_places(act, key, f):
                        ins = act.activation(d[0], d[2], ACT.Copy)
                    ins.then_inc(sem['op_hi'], 1)
                elif kind == 'vs':
                    act.wait_ge(sem['v_turned'], count['v_turned', key])
                    for name, k_ in plan.freed['V', f['dst']]:
                        act.wait_ge(sem[name], count[name, k_])
                    dst, src = v_places(key, f, 0)
                    act.activation(dst, src, ACT.Copy).then_inc(sem['v_hi'], 1)
                elif kind == 'tab':
                    k = plan.slot['tab', key]
                    for name, k_ in plan.freed['tab', key]:
                        act.wait_ge(sem[name], count[name, k_])
                    (l, _, j), i = key
                    act.wait_ge(sem['par_done'], count['par_done', DEPTH - 1])
                    act.dma_start(tab[:, k], bias_rows[l, 2 * j + i]).then_inc(s_tab[k], 16)
                elif kind == 'bias':
                    u, i = key
                    act.wait_ge(sem['bias_full'], count['bias_full', key])
                    for name, k_ in plan.freed['bias', u]:
                        act.wait_ge(sem[name], count[name, k_])
                    act.wait_ge(sem['piece_used'], count['piece_used', ((u[0], 'A', 'kv', 7), 0)])
                    act.activation(bias_r(u, i, 0), Y[:, BT_AT:BT_AT + 384], ACT.Copy).then_inc(sem['bias_hi'], 1)
                elif kind == 'ex':
                    u, h = key[0], key[1]
                    sm = small[:, plan.slot['small', key]]
                    act.wait_ge(sem['negmax_ready'], count['negmax_ready', key])
                    for name, k_ in plan.freed['P', key]:
                        act.wait_ge(sem[name], count[name, k_])
                    ss = subs(key)
                    if u[1] == 'B':
                        act.activation(sm[:, 6:6 + len(ss)], sm[:, 2:2 + len(ss)], ACT.Exp, bias=sink[:, u[0], h:h + 1])
                    for i, (a, b) in enumerate(ss):
                        ins = act.activation(prob('P', key)[:, a:b], s_bank(key)[:, a:b], ACT.Exp,
                                             bias=sm[:, 2 + i:3 + i], scale=scale_of(key), accum_out=sm[:, 4 + i:5 + i])
                    ins.then_inc(sem['exp_done'], 1)
                elif kind == 'trs':
                    act.wait_ge(sem['p_turned'], count['p_turned', key])
                    for name, k_ in plan.freed['PT', key[:3]]:
                        act.wait_ge(sem[name], count[name, k_])
                    dst, src = pt_places(key, 0)
                    act.activation(dst, src, ACT.Copy).then_inc(sem['pt_hi'], 1)
                elif kind == 'ov':
                    act.wait_ge(sem['pv_done'], count['pv_done', key])
                    dst, src, _ = o_places(key)
                    act.activation(dst, src, ACT.Copy).then_inc(sem['o_hi'], 1)
                elif kind == 'gsig':
                    n = f['n']
                    act.wait_ge(sem['piece_used'], count['piece_used', last_piece(('gate', key))])
                    for name, k_ in plan.freed['tmp', ('gate', key)]:
                        act.wait_ge(sem[name], count[name, k_])
                    act.activation(tmp[:, plan.slot['tmp', ('gate', key)], 0:n], acc(('gate', key))[:, 0:n],
                                   ACT.Sigmoid).then_inc(sem['gate_sig'], 1)
                elif kind == 'ms':
                    l, dt = key
                    n = f['n']
                    act.wait_ge(sem['gate_acc'], count['gate_acc', (l, dt, 3)])
                    act.activation(operand('M', 0, dt, n), macc(key)[:, 0:n], ACT.Copy).then_inc(sem['m_hi'], 1)
                elif kind == 'fsig':
                    n = f['n']
                    act.wait_ge(sem['piece_used'], count['piece_used', last_piece(('fa', key))])
                    for name, k_ in plan.freed['tmp', ('ffn', key)]:
                        act.wait_ge(sem[name], count[name, k_])
                    act.activation(tmp[:, plan.slot['tmp', ('ffn', key)], 0:n], acc(('fa', key))[:, 0:n],
                                   ACT.Sigmoid).then_inc(sem['ffn_sig'], 1)
                elif kind == 'fh':
                    n = f['n']
                    act.wait_ge(sem['ffn_h'], count['ffn_h', key])
                    act.activation(operand('hid', 0, key[1], n), fil[:, plan.slot['fil', ('ffn', key)], 0:n],
                                   ACT.Copy).then_inc(sem['hid_hi'], 1)
                elif kind == 'tout':
                    tt, half = key
                    act.wait_ge(sem['out_turned'], count['out_turned', key])
                    at = tt * D + half * 512
                    act.activation(Y[:, at:at + 512], acc(('tout', tt, half))[:, :], ACT.Copy)\
                        .then_inc(sem['out_copied'], 1)

        @block.vector
        def _(dve):
            dve.wait_ge(s_rows, n_rows)
            dve.tensor_scalar(sink8[:, :, :], sink[:, :, :], float(DH) ** 0.5, None, ALU.mult).then_inc(s_init, 1)
            for kind, key, f in steps:
                if kind == 'cin':
                    dve.wait_ge(sem['c_sig'], count['c_sig', key])
                    dve.tensor_tensor(crows[:, 2, :], crows[:, 0, :], crows[:, 1, :], ALU.mult)\
                        .then_inc(sem['c_silu'], 1)
                    dve.wait_ge(sem['c_turned'], count['c_turned', key])
                    dve.tensor_copy(sc[:, :, :], acc(('cin',))[:, 0:16].rearrange("p (s k) -> p s k", s=2))\
                        .then_inc(sem['c_done'], 1)
                elif kind == 'par':
                    dve.wait_ge(sem['par_turned'], count['par_turned', key])
                    dve.tensor_copy(par[:, key, :], acc(('par', key))[:, 0:ROWS]).then_inc(sem['par_done'], 1)
                elif kind == 'split':
                    sz = piece_size(tile[key[0]]['pieces'][key[1]])
                    slot = plan.slot['w', key]
                    dve.wait_ge(load_sem[landed[key][0]], landed[key][1])
                    dve.wait_ge(sem['w_hi'], count['w_hi', key])
                    for name, k_ in plan.freed['w', key]:
                        dve.wait_ge(sem[name], count[name, k_])
                    dve.tensor_tensor(w_ring[:, slot, 1, 0:sz], load_ring[:, plan.slot['load', key], 0:sz],
                                      w_ring[:, slot, 0, 0:sz].bitcast(F32), ALU.subtract).then_inc(sem['w_lo'], 1)
                elif kind == 'modadd':
                    l, ch = key
                    dve.wait_ge(sem['piece_used'], count['piece_used', last_piece(('mod', l, ch))])
                    dve.wait_ge(sem['par_done'], count['par_done', l])
                    dve.tensor_scalar(mod[:, l, ch, :], acc(('mod', l, ch))[:, 0:2], par[:, l, ch:ch + 1], None,
                                      ALU.add).then_inc(sem['mod_ready'], 1)
                elif kind == 'coef':
                    l, g = key
                    dve.wait_ge(sem['mod_ready'], count['mod_ready', (l, (15, 23, 47)[g])])

                    def gain(i):
                        return par[:, l, 48 + 8 * i:56 + 8 * i].unsqueeze(2).to_broadcast([P, KT, 2])
                    if g != 1:
                        at = (8, 0, 32)[g]
                        ins = dve.scalar_tensor_tensor(out=coef[:, l, g], in0=mod[:, l, at:at + 8, :], scalar=1.0,
                                                       in1=gain(g), op0=ALU.add, op1=ALU.mult)
                    if g:
                        at = (0, 16, 40)[g]
                        ins = dve.tensor_tensor(coef[:, l, 2 * g - 1], mod[:, l, at:at + 8, :], gain(2 * g - 1), ALU.mult)
                    ins.then_inc(sem['coef_ready'], 1)
                elif kind == 'stat':
                    m = f['n'] // P * f['nh']
                    dve.wait_ge(sem['stat_sum'], count['stat_sum', key])
                    if count['stat_mean', key] > 1:
                        dve.wait_ge(sem['stat_rstd'], count['stat_rstd', key] - 1)
                    dve.tensor_scalar(stat[:, 0, 0:m], acc(('stat', key))[:, 0:m], 1.0 / f['dim'], EPS, ALU.mult,
                                      ALU.add).then_inc(sem['stat_mean'], 1)
                    dve.wait_ge(sem['stat_rstd'], count['stat_rstd', key])
                    if count['rstd_bcast', key] > 1:
                        dve.wait_ge(sem['rstd_bcast'], count['rstd_bcast', key] - 1)
                    w = P // f['nh']
                    dve.tensor_copy(wide[:, 0:f['n']].rearrange("p (m w) -> p m w", w=w),
                                    stat[:, 1, 0:m].unsqueeze(2).to_broadcast([P, m, w])).then_inc(sem['stat_wide'], 1)
                elif kind == 'apA':
                    nm, kt = key
                    k2 = ('ap', nm, kt)
                    n = f['n']
                    dve.wait_ge(sem['rstd_bcast'], count['rstd_bcast', nm])
                    for name, k_ in plan.freed['tmp', k2]:
                        dve.wait_ge(sem[name], count[name, k_])
                    dve.tensor_tensor(tmp[:, plan.slot['tmp', k2], 0:n], H[:, kt, 0:n], acc(('bc', nm))[:, 0:n],
                                      ALU.mult).then_inc(sem['ap_scaled'], 1)
                elif kind == 'apB':
                    nm, kt = key
                    n = f['n']
                    dve.wait_ge(sem['ap_hi'], count['ap_hi', key])
                    dve.wait_ge(sem['ap_full'], count['ap_full', key])
                    dve.tensor_tensor(U[1][:, kt, 0:n], fil[:, plan.slot['fil', ('ap', nm, kt)], 0:n],
                                      U[0][:, kt, 0:n].bitcast(F32), ALU.subtract).then_inc(sem['ap_lo'], 1)
                elif kind == 'post':
                    nm, kt = key
                    n = f['n']
                    k2 = ('post', nm, kt)
                    dve.wait_ge(sem['rstd_bcast'], count['rstd_bcast', nm])
                    dve.wait_ge(sem['y_ready'], count['y_ready', key])
                    for name, k_ in plan.freed['tmp', k2]:
                        dve.wait_ge(sem[name], count[name, k_])
                    dve.tensor_tensor(tmp[:, plan.slot['tmp', k2], 0:n], y_tile(kt)[:, 0:n], acc(('bc', nm))[:, 0:n],
                                      ALU.mult).then_inc(sem['post_scaled'], 1)
                elif kind == 'posth':
                    nm, kt = key
                    dve.wait_ge(sem['post_scaled'], count['post_scaled', key])
                    dve.wait_ge(sem['coef_ready'], count['coef_ready', (f['l'], 1 + f['which'])])
                    for side in range(f['n'] // SEQ):
                        r = slice(side * SEQ, (side + 1) * SEQ)
                        ins = dve.scalar_tensor_tensor(
                            out=H[:, kt, r], in0=tmp[:, plan.slot['tmp', ('post', nm, kt)], r],
                            scalar=coef[:, f['l'], 1 + 2 * f['which'], kt, side:side + 1], in1=H[:, kt, r],
                            op0=ALU.mult, op1=ALU.add)
                    ins.then_inc(sem['h_new'], 1)
                elif kind == 'gn':
                    n = f['n']
                    l, col = f['g']
                    dve.wait_ge(sem['rstd_bcast'], count['rstd_bcast', f['bc']])
                    dve.wait_ge(sem['raw_ready'], count['raw_ready', key])
                    dve.scalar_tensor_tensor(out=raw(key)[:, 0:n], in0=raw(key)[:, 0:n], scalar=par[:, l, col:col + 1],
                                             in1=acc(('bc', f['bc']))[:, 0:n], op0=ALU.mult,
                                             op1=ALU.mult).then_inc(sem['normed'], 1)
                elif kind == 'rope':
                    r = f['rows']
                    t = tmp[0:r, plan.slot['tmp', ('rope', key)], 0:SEQ]
                    dve.wait_ge(sem['rotated'], count['rotated', key])
                    for name, k_ in plan.freed['tmp', ('rope', key)]:
                        dve.wait_ge(sem[name], count[name, k_])
                    dve.tensor_tensor(t, acc(('rot', key))[0:r, 0:SEQ], const('sin' + f['t'], r),
                                      ALU.mult).then_inc(sem['rope_sin'], 1)
                    dve.wait_ge(sem['rope_sin'], count['rope_sin', key])
                    dve.wait_ge(sem['rope_cos'], count['rope_cos', key])
                    dve.tensor_tensor(raw(key)[0:r, 0:SEQ], raw(key)[0:r, 0:SEQ], t, ALU.add)\
                        .then_inc(sem['roped'], 1)
                elif kind == 'qks':
                    places = split_places(dve, key, f)
                    dve.wait_ge(sem['op_hi'], count['op_hi', key])
                    for hi, lo, src in places:
                        ins = dve.tensor_tensor(lo, src, hi.bitcast(F32), ALU.subtract)
                    ins.then_inc(sem['op_lo'], 1)
                elif kind == 'vs':
                    dve.wait_ge(sem['v_hi'], count['v_hi', key])
                    dst, src = v_places(key, f, 1)
                    hi, _ = v_places(key, f, 0)
                    dve.tensor_tensor(dst, src, hi.bitcast(F32), ALU.subtract).then_inc(sem['v_lo'], 1)
                elif kind == 'bias':
                    u, i = key
                    k = plan.slot['tab', key]
                    dve.wait_ge(s_tab[k], 16 * ((count['bias_full', key] + 1) // 2))
                    if count['bias_full', key] > 1:
                        dve.wait_ge(sem['bias_lo'], count['bias_lo', key] - 1)
                    dve.scalar_tensor_tensor(
                        out=Y[:, BT_AT:BT_AT + 384].rearrange("p (j c) -> p j c", j=6),
                        in0=tab[:, k, :].rearrange("p (j c) -> p j c", j=6), scalar=float(DH) ** 0.5,
                        in1=const('maskC').unsqueeze(1).to_broadcast([P, 6, GRID]), op0=ALU.mult,
                        op1=ALU.add).then_inc(sem['bias_full'], 1)
                elif kind == 'mx':
                    u, h = key[0], key[1]
                    sm = small[:, plan.slot['small', key]]
                    ss = subs(key)
                    m = len(ss)
                    dve.wait_ge(sem['scores'], count['scores', key])
                    for name, k_ in plan.freed['small', key]:
                        dve.wait_ge(sem[name], count[name, k_])
                    dve.tensor_reduce(sm[:, 0:m], s_bank(key)[:, :].rearrange("p (m k) -> p m k", m=m), AX_X,
                                      ALU.max).then_inc(sem['max_ready'], 1)
                    dve.wait_ge(sem['max_ready'], count['max_ready', key])
                    if u[1] == 'B':
                        dve.tensor_scalar(sm[:, 2:2 + m], sm[:, 0:m], sink8[:, u[0], h:h + 1], -scale_of(key), ALU.max,
                                          ALU.mult).then_inc(sem['negmax_ready'], 1)
                    else:
                        dve.tensor_scalar(sm[:, 2:2 + m], sm[:, 0:m], -scale_of(key), None,
                                          ALU.mult).then_inc(sem['negmax_ready'], 1)
                elif kind == 'sinksum':
                    sm = small[:, plan.slot['small', key]]
                    m = len(subs(key))
                    dve.wait_ge(sem['exp_done'], count['exp_done', key])
                    dve.tensor_tensor(sm[:, 8:8 + m], sm[:, 4:4 + m], sm[:, 6:6 + m], ALU.add)\
                        .then_inc(sem['sum_ready'], 1)
                elif kind == 'den':
                    sm = small[:, plan.slot['small', key]]
                    m = len(subs(key))
                    dve.wait_ge(sem['exp_done'], count['exp_done', key])
                    at = 4
                    if key[0][1] == 'B':
                        dve.wait_ge(sem['sum_ready'], count['sum_ready', key])
                        at = 8
                    dve.reciprocal(sm[:, 10:10 + m], sm[:, at:at + m]).then_inc(sem['rec_ready'], 1)
                elif kind == 'trs':
                    dve.wait_ge(sem['pt_hi'], count['pt_hi', key])
                    dst, src = pt_places(key, 1)
                    hi, _ = pt_places(key, 0)
                    dve.tensor_tensor(dst, src, hi.bitcast(F32), ALU.subtract).then_inc(sem['pt_lo'], 1)
                elif kind == 'ov':
                    dve.wait_ge(sem['o_hi'], count['o_hi', key])
                    hi, src, lo = o_places(key)
                    dve.tensor_tensor(lo, src, hi.bitcast(F32), ALU.subtract).then_inc(sem['o_lo'], 1)
                elif kind == 'gmul':
                    l, dt, n_ = key
                    n = f['n']
                    dve.wait_ge(sem['gate_sig'], count['gate_sig', key])
                    dve.wait_ge(sem['piece_used'], count['piece_used', last_piece(('up', key))])
                    if n_:
                        for name, k_ in plan.freed['fil', ('gate', key)]:
                            dve.wait_ge(sem[name], count[name, k_])
                        dst = fil[:, plan.slot['fil', ('gate', key)], 0:n]
                    else:
                        for name, k_ in plan.freed['macc', (l, dt)]:
                            dve.wait_ge(sem[name], count[name, k_])
                        dst = macc((l, dt))[:, 0:n]
                    dve.tensor_tensor(dst, tmp[:, plan.slot['tmp', ('gate', key)], 0:n], acc(('up', key))[:, 0:n],
                                      ALU.mult).then_inc(sem['gate_mul'], 1)
                elif kind == 'ms':
                    l, dt = key
                    n = f['n']
                    dve.wait_ge(sem['m_hi'], count['m_hi', key])
                    dve.tensor_tensor(operand('M', 1, dt, n), macc(key)[:, 0:n], operand('M', 0, dt, n).bitcast(F32),
                                      ALU.subtract).then_inc(sem['m_lo'], 1)
                elif kind == 'fsig':
                    n = f['n']
                    t = tmp[:, plan.slot['tmp', ('ffn', key)], 0:n]
                    dve.wait_ge(sem['ffn_sig'], count['ffn_sig', key])
                    dve.tensor_tensor(t, t, acc(('fa', key))[:, 0:n], ALU.mult).then_inc(sem['ffn_silu'], 1)
                elif kind == 'fh':
                    n = f['n']
                    dve.wait_ge(sem['ffn_silu'], count['ffn_silu', key])
                    dve.wait_ge(sem['piece_used'], count['piece_used', last_piece(('fb', key))])
                    for name, k_ in plan.freed['fil', ('ffn', key)]:
                        dve.wait_ge(sem[name], count[name, k_])
                    dve.tensor_tensor(fil[:, plan.slot['fil', ('ffn', key)], 0:n],
                                      tmp[:, plan.slot['tmp', ('ffn', key)], 0:n], acc(('fb', key))[:, 0:n],
                                      ALU.mult).then_inc(sem['ffn_h'], 1)

        @block.tensor
        def _(pe):
            pe.wait_ge(s_const, 16)
            pe.wait_ge(s_init, 3)

            def three(dst, lhs, rhs, start, stop):
                pe.matmul(dst, lhs[0], rhs[0], start=start, stop=False)
                pe.matmul(dst, lhs[0], rhs[1], start=False, stop=False)
                return pe.matmul(dst, lhs[1], rhs[0], start=False, stop=stop)

            for kind, key, f in steps:
                if kind == 'cin':
                    pe.wait_ge(sem['c_silu'], count['c_silu', key])
                    pe.transpose(acc(('cin',))[:, 0:16], crows[:, 2, :], ident[0:16, 0:16]).then_inc(sem['c_turned'], 1)
                elif kind == 'par':
                    for name, k_ in plan.freed['acc', ('par', key)]:
                        pe.wait_ge(sem[name], count[name, k_])
                    pe.transpose(acc(('par', key))[:, 0:ROWS], rows[0:ROWS, key, :], ident[0:ROWS, 0:ROWS])\
                        .then_inc(sem['par_turned'], 1)
                elif kind == 'xin':
                    if key == 0:
                        pe.wait_ge(s_x, 32)
                    for name, k_ in plan.freed['acc', ('xin', key)]:
                        pe.wait_ge(sem[name], count[name, k_])
                    for tt in range(NTOK // P):
                        at = tt * D + key * P
                        ins = pe.transpose(acc(('xin', key))[:, tt * P:(tt + 1) * P], Y[:, at:at + P], ident)
                    ins.then_inc(sem['xin_turned'], 1)
                elif kind == 'mm':
                    t, j = key
                    g = tile[t]
                    m, n = g['rows'], g['n']
                    if j == 0:
                        for name, k_ in plan.freed['acc', t]:
                            pe.wait_ge(sem[name], count[name, k_])
                    for name, k in (g['need'].get(j, ()) if g['need'] else ()):
                        pe.wait_ge(sem[name], count[name, k])
                    kts = list(g['kt'](j))
                    lastp = j == len(g['pieces']) - 1
                    if g['exact']:
                        pe.wait_ge(load_sem[landed[key][0]], landed[key][1])
                        pe.wait_ge(sem['c_done'], count['c_done', 0])
                    else:
                        pe.wait_ge(sem['w_hi'], count['w_hi', key])
                        pe.wait_ge(sem['w_lo'], count['w_lo', key])
                    for i, kt in enumerate(kts):
                        start, stop = j == 0 and i == 0, lastp and i == len(kts) - 1
                        dst = acc(t)[0:m, 0:n]
                        if g['exact']:
                            ins = pe.matmul(dst, w_slice(key, None, i), sc[:, :, kt], start=start, stop=stop)
                        else:
                            ins = three(dst, [w_slice(key, a, i) for a in range(2)],
                                        [operand(g['src'], a, kt, n) for a in range(2)], start, stop)
                    ins.then_inc(sem['piece_used'], 1)
                elif kind == 'stat':
                    nh = f['nh']
                    for name, k_ in plan.freed['acc', ('stat', key)]:
                        pe.wait_ge(sem[name], count[name, k_])
                    if f['srcs'] is None:
                        pe.wait_ge(sem['sq_sum'], count['sq_sum', (key, KT - 1)])
                        srcs = [sqacc]
                    else:
                        for k in f['srcs']:
                            pe.wait_ge(sem['rawsq_ready'], count['rawsq_ready', k])
                        srcs = [fil[:, plan.slot['fil', k], :] for k in f['srcs']]
                    ones = const('ones') if nh == 1 else const('halves')
                    for tt in range(f['n'] // P):
                        for i, s in enumerate(srcs):
                            ins = pe.matmul(acc(('stat', key))[:, tt * nh:(tt + 1) * nh], s[:, tt * P:(tt + 1) * P], ones,
                                            start=i == 0, stop=i == len(srcs) - 1)
                    ins.then_inc(sem['stat_sum'], 1)
                elif kind == 'bcast':
                    for name, k_ in plan.freed['acc', ('bc', key)]:
                        pe.wait_ge(sem[name], count[name, k_])
                    pe.wait_ge(sem['stat_wide'], count['stat_wide', key])
                    for tt in range(f['n'] // P):
                        ins = pe.matmul(acc(('bc', key))[:, tt * P:(tt + 1) * P], wide[:, tt * P:(tt + 1) * P], ident,
                                        start=True, stop=True)
                    ins.then_inc(sem['rstd_bcast'], 1)
                elif kind == 'rot':
                    r = f['rows']
                    for name, k_ in plan.freed['acc', ('rot', key)]:
                        pe.wait_ge(sem[name], count[name, k_])
                    pe.wait_ge(sem['normed' if f['normed'] else 'raw_ready'], count['normed' if f['normed'] else 'raw_ready', key])
                    pe.matmul(acc(('rot', key))[0:r, 0:SEQ], const('rot' + f['t'], r)[:, 0:r], raw(key)[0:r, 0:SEQ],
                              start=True, stop=True).then_inc(sem['rotated'], 1)
                elif kind == 'vtr':
                    w = f['wide']
                    for name, k_ in plan.freed['acc', ('vtr', key)]:
                        pe.wait_ge(sem[name], count[name, k_])
                    pe.wait_ge(sem['raw_ready'], count['raw_ready', key])
                    for tt in range(4):
                        ins = pe.transpose(acc(('vtr', key))[:, tt * w:(tt + 1) * w],
                                           raw(key)[P - w:P, tt * P:(tt + 1) * P], ident[P - w:P, P - w:P])
                    ins.then_inc(sem['v_turned'], 1)
                elif kind == 'sc':
                    u, h, side, qt = key
                    l, b, j = u
                    gen = plan.kgen[u]
                    pe.wait_ge(sem['op_lo'], count['op_lo', (l, b, 'q', j)])
                    pe.wait_ge(sem['op_lo'], count['op_lo', (l, 'A', 'kv', j) if b == 'A' else (l, b, 'k', gen[2])])
                    for name, k_ in plan.freed['S', key]:
                        pe.wait_ge(sem[name], count[name, k_])
                    if b == 'A':
                        pe.wait_ge(sem['op_lo'], count['op_lo', (l, 'kr')])
                        d0, d1 = 0, DA
                    else:
                        d0 = (h // 4 if b in 'BD' else h % 2) * DH
                        d1 = d0 + DH
                    q = [staged('Q', u, a)[d0:d1, :] for a in range(2)]
                    k = [staged('K', gen, a)[d0:d1, :] for a in range(2)]
                    s = s_bank(key)
                    if side == 'x':
                        biased = b in 'BC'
                        ins = three(s[:, :], [x_[:, qt * P:(qt + 1) * P] for x_ in q], k, True, not biased)
                        if b == 'B':
                            ins = pe.matmul(s[:, 0:SEQ], ident_r[:, :], mask_r[:, qt * SEQ:(qt + 1) * SEQ], start=False,
                                            stop=True)
                        if b == 'C':
                            i = h % 2
                            pe.wait_ge(sem['bias_lo'], count['bias_lo', (u, i)])
                            at = (2 - 2 * qt) * GRID
                            pe.matmul(s[:, 0:SEQ], ident_r[:, :], bias_r(u, i, 0)[:, at:at + SEQ], start=False, stop=False)
                            ins = pe.matmul(s[:, 0:SEQ], ident_r[:, :], bias_r(u, i, 1)[:, at:at + SEQ], start=False,
                                            stop=True)
                    else:
                        for t in range(2):
                            ins = three(s[:, t * CTX:(t + 1) * CTX], [x_[:, SEQ + t * P:SEQ + (t + 1) * P] for x_ in q],
                                        [x_[:, SEQ:NTOK] for x_ in k], True, True)
                    ins.then_inc(sem['scores'], 1)
                elif kind == 'tr':
                    for name, k_ in plan.freed['T', key]:
                        pe.wait_ge(sem[name], count[name, k_])
                    pe.wait_ge(sem['prob_ready'], count['prob_ready', key])
                    for i in range(4):
                        ins = pe.transpose(t_bank(key)[:, i * P:(i + 1) * P], prob('Pn', key)[:, i * P:(i + 1) * P], ident)
                    ins.then_inc(sem['p_turned'], 1)
                elif kind == 'pv':
                    u, h, side = key
                    for name, k_ in plan.freed['pv', key]:
                        pe.wait_ge(sem[name], count[name, k_])
                    gen = plan.kgen[u]
                    vkey = (u[0], 'A', 'kv', u[2]) if u[1] == 'A' else (u[0], u[1], 'v', gen[2])
                    pe.wait_ge(sem['v_lo'], count['v_lo', vkey])
                    pe.wait_ge(sem['pt_lo'], count['pt_lo', (u, h, side, 1 if side == 'x' else 0)])
                    c0 = v_column(u, h)
                    v = [staged('V', gen, a).rearrange("p (t w) -> p t w", t=4)[:, :, c0:c0 + DH] for a in range(2)]
                    tiles = range(4) if side == 'x' else range(2, 4)
                    for i, kt in enumerate(tiles):
                        ins = three(pv_bank[0:DH, 0:SEQ], [a[:, kt, :] for a in v],
                                    [pt(key, a)[:, i, :] for a in range(2)], i == 0, i == len(tiles) - 1)
                    ins.then_inc(sem['pv_done'], 1)
                elif kind == 'tout':
                    tt, half = key
                    for name, k_ in plan.freed['acc', ('tout', tt, half)]:
                        pe.wait_ge(sem[name], count[name, k_])
                    for i in range(4):
                        kt = 4 * half + i
                        pe.wait_ge(sem['h_new'], count['h_new', ((DEPTH - 1, 'post_ffn'), kt)])
                        ins = pe.transpose(acc(('tout', tt, half))[:, i * P:(i + 1) * P], H[:, kt, tt * P:(tt + 1) * P],
                                           ident)
                    ins.then_inc(sem['out_turned'], 1)


def constant_table():
    t = np.zeros((P, NCONST), np.float32)

    def put(name, v):
        t[:v.shape[0], CONST[name][0]:CONST[name][0] + v.shape[1]] = v
    tok = np.arange(SEQ)

    def rope(d, rows_):
        half = d // 2
        inv = 10000.0 ** (-np.arange(half // 2, dtype=np.float64) * 2.0 / half)
        cos, sin, rot = np.ones((d, SEQ)), np.zeros((d, SEQ)), np.zeros((d, d))
        for ax, pos in enumerate((tok // GRID, tok % GRID)):
            ang = inv.astype(np.float32)[:, None] * pos.astype(np.float32)[None, :]
            for k in range(2):
                r = slice(ax * half + k * (half // 2), ax * half + (k + 1) * (half // 2))
                cos[r], sin[r] = np.cos(ang), np.sin(ang)
            for i in range(half // 2):
                a, b = ax * half + i, ax * half + half // 2 + i
                rot[b, a], rot[a, b] = -1.0, 1.0
        return cos, sin, rot
    cos, sin, rot = rope(DH, P)
    put('cosB', np.concatenate([cos, cos]))
    put('sinB', np.concatenate([sin, sin]))
    put('rotB', np.kron(np.eye(2), rot))
    cos, sin, rot = rope(ROPE, DA)
    put('cosA', np.concatenate([np.ones((NOPE, SEQ)), cos]))
    put('sinA', np.concatenate([np.zeros((NOPE, SEQ)), sin]))
    r = np.zeros((DA, DA))
    r[NOPE:, NOPE:] = rot
    put('rotA', r)
    put('ident', np.eye(P))
    q = np.arange(SEQ)
    m = np.where(np.abs(q[:, None] - q[None, :]) <= 128, 0.0, NEG)
    put('maskB', np.concatenate([m[0:P], m[P:]], axis=1))
    qc = np.arange(P) % GRID
    c0 = np.clip(qc - KWIN // 2, 0, GRID - KWIN)
    kc = np.arange(GRID)
    put('maskC', np.where((kc[None] >= c0[:, None]) & (kc[None] < c0[:, None] + KWIN), 0.0, NEG))
    put('halves', np.kron(np.eye(2), np.ones((DH, 1))))
    put('ones', np.ones((P, 1)))
    put('power', np.full((P, 8), -0.5))
    return t


def bias_layout(rpb):
    a = np.arange(P)[:, None, None] // GRID
    qc = np.arange(P)[:, None, None] % GRID
    j = np.arange(6)[None, :, None]
    kc = np.arange(GRID)[None, None, :]
    dr = j - 2 - a + 7 + 0 * kc
    dc = np.clip(kc - qc, -(KWIN - 1), KWIN - 1) + (KWIN - 1) + 0 * j
    return np.ascontiguousarray(rpb[:, :, dr, dc].reshape(rpb.shape[0], rpb.shape[1], P, 6 * GRID))


_INS = ['x', 'c', 'ctx', 'c_ctx', 'w_mod', 'b_mod', 'g_pre_mix', 'g_post_mix', 'g_pre_ffn', 'g_post_ffn', 'w_in',
        'g_a_q', 'g_a_kv', 'w_a_uq', 'w_a_ukv', 'sink_b', 'rpb_c', 'g_d_q', 'g_d_k', 'w_branch', 'w_out', 'w_ffn_in',
        'w_ffn_out']


def kernel(**inputs):
    import concourse.bacc as bacc
    from concourse.bass_utils import run_bass_kernel_spmd as run

    nc = bacc.Bacc("TRN2", target_bir_lowering=False, num_devices=1, dynamic_dma_scratch_size=512)
    arrays, args = {}, []
    for name in _INS:
        a = np.asarray(inputs[name])
        a = bias_layout(a) if name == 'rpb_c' else np.ascontiguousarray(a)
        arrays[f"in_{name}"] = a
        args.append(nc.dram_tensor(f"in_{name}", a.shape, mybir.dt.from_np(a.dtype), kind="ExternalInput").ap())
    arrays["in_consts"] = constant_table()
    args.append(nc.dram_tensor("in_consts", (P, NCONST), F32, kind="ExternalInput").ap())
    out = nc.dram_tensor("out_0", (1, SEQ, D), F32, kind="ExternalOutput").ap()
    build(nc, *args, out)
    r = run(nc, [arrays], core_ids=[0])
    return r.results[0]["out_0"]
```

```python
from contextlib import ExitStack

import numpy as np
import concourse.bass as bass
from concourse import mybir

ALU = mybir.AluOpType
ACT = mybir.ActivationFunctionType
F32 = mybir.dt.float32
F32R = mybir.dt.float32r
AX_X = mybir.AxisListType.X

P = 128
DEPTH, D, SEQ, CTX, DFF, DH = 2, 1024, 256, 256, 2816, 64
NTOK = SEQ + CTX
KT = D // P
GRID = 64
KWIN = 16
EPS = 1e-6
NEG = -1e30
QL, KVL, NOPE, ROPE = 256, 128, 64, 32
DA = NOPE + ROPE
WIDTHS = (('a_cq', QL), ('a_ckv', KVL), ('a_kr', ROPE), ('b_q', 512), ('b_k', 128), ('b_v', 128),
          ('c_q', 512), ('c_k', 512), ('c_v', 512), ('d_q', 512), ('d_k', 128), ('d_v', 128), ('gate', 4 * D))
OFF = {}
for _n, _w in WIDTHS:
    OFF[_n] = sum(w for _, w in WIDTHS[:len(OFF)])
FT = DFF // P
PIECE = 512
W_RING = 5
L_RING = 4
EX_AT = (1, 3, 3, 3)
MOD_RATE = (1.45, 2.0)
AHEAD = 4
MOD_COLS = 256
MOD0 = 16 * P
MOD0_POOL, MOD0_DVE = 2 * P, 11 * P
ROWS = 85

CONST = {}
for _n, _w in (('ident', 128), ('ones', 1), ('power', 8), ('rotB', 128), ('rotA', 128), ('cosB', 256), ('sinB', 256),
               ('cosA', 256), ('sinA', 256), ('maskC', 64), ('halves', 2), ('maskB', 512)):
    CONST[_n] = (CONST[_p][1] if CONST else 0, (CONST[_p][1] if CONST else 0) + _w)
    _p = _n
NFIRST, NKEPT, NCONST = CONST['power'][1], CONST['halves'][1], CONST['maskB'][1]

O_HI, O_LO, Q_AT, K_AT, V_AT, PT_AT = 0, 8192, 16384, 18432, 20480, 22528
ARENA = PT_AT + 4096
M_HI, M_LO = Q_AT, Q_AT + KT * NTOK
H_HI, H_LO = 0, FT * NTOK
CQ_HI, CQ_LO, CKV_HI, CKV_LO = O_HI + 6144, O_HI + 7168, O_LO + 6144, O_LO + 6656
BIAS_AT = (O_HI, O_LO)
QUARTER = 4 * NTOK
RAW_AT, P_AT, PN_AT, BT_AT = 0, 1536, 2560, 3584
FARENA = 4096

RINGS = {'acc': 3, 'raw': 3, 'tmp': 2, 'fil': 2, 'sig': 1, 'Q': 2, 'K': 2, 'V': 2, 'S': 2, 'P': 2, 'Pn': 2, 'T': 1,
         'PT': 2, 'pv': 1, 'w': W_RING, 'load': L_RING, 'merge': 1, 'bias': 2, 'tab': 2, 'small': 2, 'mod': 2}

SIGNALS = {
    'xin': ('xin_turned', 'xin_done'), 'cin': ('c_sig', 'c_silu', 'c_turned', 'c_done'),
    'par': ('par_turned', 'par_done'), 'mm': ('piece_used',), 'split': ('w_hi',),
    'mod0': ('mod0_mult', 'mod0_pool', 'mod0_dve', 'mod0_pe'), 'mod0sum': ('mod0_sum',), 'init': (),
    'modw': ('mod_first', 'mod_acc'), 'modsum': ('mod_sum',), 'modadd': ('mod_ready',), 'coef': ('coef_ready',),
    'sq': ('sq_done',), 'sqmm': ('sq_summed',), 'mstat': ('stat_mean', 'stat_rstd', 'stat_wide'),
    'stat': ('stat_sum', 'stat_mean', 'stat_rstd', 'stat_wide'),
    'bcast': ('rstd_bcast',), 'apA': ('ap_scaled', 'ap_hi', 'ap_full'), 'apB': ('ap_lo',),
    'post': ('post_scaled',), 'posth': ('h_new',),
    'evac': ('raw_ready',), 'evacsq': ('rawsq_ready',), 'gn': ('normed',), 'rot': ('rotated',),
    'rope': ('rope_sin', 'rope_cos', 'roped'), 'qks': ('op_hi', 'op_lo'), 'vtr': ('v_turned',), 'vs': ('v_hi', 'v_lo'),
    'tab': (), 'bias': ('bias_full', 'bias_hi', 'bias_lo'),
    'sc': ('scores',), 'mx': ('max_ready', 'negmax_ready'), 'ex': ('exp_done',),
    'sinksum': ('sum_ready',), 'den': ('rec_ready', 'prob_ready'),
    'tr': ('p_turned',), 'trs': ('pt_hi', 'pt_lo'), 'pv': ('pv_done',), 'ov': ('o_hi', 'o_lo'),
    'gsig': ('gate_tanh',), 'gmul': ('gate_mul',), 'gacc': ('gate_acc',), 'ms': ('m_hi', 'm_lo'),
    'yev': ('y_ready',), 'fsig': ('ffn_sig', 'ffn_silu'), 'fh': ('ffn_h', 'hid_hi', 'hid_lo'),
    'tout': ('out_turned', 'out_copied'),
}


class ModPlan:

    def __init__(self, p):
        self.p, self.owed, self.todo, self.per = p, 0.0, [], MOD_COLS // P
        self.fresh, self.free_after, self.layer = 0, None, 0
        for l, chunks in ((0, range(MOD0 // P, 48, self.per)), (1, range(0, 48, self.per))):
            for ch in chunks:
                self.todo += [('modw', (l, ch), j) for j in range(KT // 2)] + [('modsum', (l, ch), 0)]

    def enter(self, layer, free_after):
        self.layer = layer
        self.fresh, self.free_after = RINGS['mod'], free_after

    def rest(self, l):
        while self.todo and self.todo[0][1][0] <= l:
            self.some(1)
        self.p.mods_done.append([key for kind, key, _ in self.p.steps if kind == 'modw'][-1])

    def some(self, rate):
        p, first = self.p, True
        self.owed += rate
        while self.todo and self.todo[0][1][0] == self.layer and self.owed >= 1:
            kind, key, j = self.todo[0]
            if kind == 'modsum' and not first:
                break
            self.todo.pop(0)
            self.owed -= 1
            first = False
            l, ch = key
            sides = 2 if l == 0 or ch < 16 else 1
            if kind == 'modw':
                if self.fresh:
                    p.mod_after[key, j] = self.free_after
                    self.fresh -= 1
                p.take('mod', (key, j), ('mod_acc', (key, j)))
                p.step('modw', (key, j), sides=sides)
            else:
                p.take('acc' if l else 'pv', ('mod', key), ('mod_ready', key))
                p.step('modsum', key, sides=sides)
                p.step('modadd', key, first=ch, chunks=self.per, sides=sides)
                if l == 0 and ch + self.per in (24, 48):
                    p.step('coef', (0, 1 if ch < 24 else 2))


class Plan:

    def __init__(self):
        self.steps, self.tile = [], {}
        self.slot, self.freed, self.users = {}, {}, {r: [] for r in RINGS}
        self.kgen, self.last_main, self.before = {}, None, {}
        self.mod_after, self.mods_done = {}, []
        self.loads, self.lo, self.on_pool = [], {}, set()

    def step(self, kind, key, **facts):
        self.steps.append((kind, key, facts))

    def take(self, ring, key, *frees):
        users = self.users[ring]
        n = RINGS[ring]
        self.slot[ring, key] = len(users) % n
        self.freed[ring, key] = users[-n] if len(users) >= n else ()
        users.append(frees)

    def gemm(self, key, pieces, src, kt_of, rows, n, frees, need=(), ring='acc'):
        self.take(ring, key, *frees)
        self.tile[key] = dict(pieces=pieces, src=src, kt=kt_of, rows=rows, n=n, need=need, ring=ring)
        out = []
        for j, _ in enumerate(pieces):
            out.append(('mm', (key, j), {}))
        return out


def win_pieces(l, name, c0, cols=P, halves=None):
    starts = [OFF[name] + h * DH for h in halves] if halves else [OFF[name] + c0]
    return [dict(w='w_in', l=l, row=4 * j, nk=4, cols=cols, starts=starts) for j in range(2)]


def build_plan():
    p = Plan()
    S = p.steps

    def norm_stat(nm, srcs, nh, dim, n, frees):
        if srcs is None:
            p.step('mstat', nm, nh=1, dim=dim, n=n)
        else:
            p.take('acc', ('stat', nm), ('stat_mean', nm))
            p.step('stat', nm, srcs=srcs, nh=nh, dim=dim, n=n)
        p.take('acc', ('bc', nm), *frees)
        p.step('bcast', nm, n=n)

    def square(nm, kt, n, what, made):
        p.take('fil', ('sq', nm, kt), ('sq_summed', (nm, kt)))
        if kt == 0:
            p.before[nm], p.last_main = p.last_main, nm
        p.step('sq', (nm, kt), n=n, what=what, made=made)

    def square_sum(nm, kt, n):
        p.step('sqmm', (nm, kt), n=n)

    def apply(nm, l, which, n):
        for kt in range(KT + 1):
            if kt < KT:
                p.take('tmp', ('ap', nm, kt), ('ap_hi', (nm, kt)), ('ap_full', (nm, kt)))
                p.take('fil', ('ap', nm, kt), ('ap_lo', (nm, kt)))
                p.step('apA', (nm, kt), l=l, which=which, n=n)
            if kt:
                p.step('apB', (nm, kt - 1), n=n)

    def post(nm, l, which, n, then):
        for kt in range(KT + 1):
            if kt < KT:
                p.take('tmp', ('post', nm, kt), ('h_new', (nm, kt)))
                p.step('post', (nm, kt), n=n)
            if kt:
                p.step('posth', (nm, kt - 1), l=l, which=which, n=n)
                if then:
                    square(then, kt - 1, n, 'H', ('h_new', (nm, kt - 1)))
                    square_sum(then, kt - 1, n)

    p.take('acc', ('cin',), ('c_done', 0))
    p.step('cin', 0)
    p.step('mod0', 0)
    for kt in range(KT):
        p.take('acc', ('xin', kt), ('xin_done', kt))
        p.step('xin', kt)
        square((0, 'pre_mix'), kt, NTOK, 'H', ('xin_done', kt))
        if kt:
            square_sum((0, 'pre_mix'), kt - 1, NTOK)
            p.step('mod0', kt)
    square_sum((0, 'pre_mix'), KT - 1, NTOK)
    p.step('init', 0)
    for l in range(DEPTH):
        p.take('acc', ('par', l), ('par_done', l))
        p.step('par', l)
    p.step('mod0sum', 0)
    p.step('modadd', (0, 0), first=0, chunks=MOD0 // P, sides=2)
    p.step('coef', (0, 0))
    mods = ModPlan(p)
    mods.enter(0, ('coef', 'coef_ready', (0, 0)))

    for l in range(DEPTH):
        last = l == DEPTH - 1
        nq = SEQ if last else NTOK
        nm = (l, 'pre_mix')
        norm_stat(nm, None, 1, D, NTOK, [('ap_scaled', (nm, KT - 1))])
        apply(nm, l, 0, NTOK)
        need_u = {0: [('ap_lo', (nm, 3))], 1: [('ap_lo', (nm, 7))]}

        def proj(name, key, n, c0=0, cols=P, halves=None, frees=(), need=None):
            return p.gemm(key, win_pieces(l, name, c0, cols, halves), 'U', lambda j: range(4 * j, 4 * j + 4), cols, n,
                          frees, need or {})

        ckv, kr, cq = (l, 'ckv'), (l, 'kr'), [(l, 'cq', 0), (l, 'cq', 1)]
        S.extend(proj('a_ckv', ckv, NTOK, frees=[('rawsq_ready', ckv)], need=need_u))
        p.take('raw', ckv, ('op_hi', ckv), ('op_lo', ckv))
        p.take('fil', ckv, ('stat_sum', ckv))
        p.step('evac', ckv, rows=(0, P), n=NTOK)
        p.step('evacsq', ckv, rows=(0, P), n=NTOK)
        for t, k in enumerate(cq):
            S.extend(proj('a_cq', k, nq, c0=t * P, frees=[('rawsq_ready', k)]))
            if t == 0:
                norm_stat(ckv, [ckv], 1, KVL, NTOK, [('normed', ckv)])
                p.step('gn', ckv, bc=ckv, n=NTOK, g=(l, 82))
                p.step('qks', ckv, src='raw', rows=(0, P), n=NTOK, dst=('ckv', 0))
            p.take('raw', k, ('op_hi', k), ('op_lo', k))
            p.take('fil', k, ('stat_sum', cq[1]))
            p.step('evac', k, rows=(0, P), n=nq)
            p.step('evacsq', k, rows=(0, P), n=nq)
        S.extend(proj('a_kr', kr, NTOK, c0=-NOPE, cols=DA, frees=[('raw_ready', kr)]))
        norm_stat(cq[1], cq, 1, QL, nq, [('normed', cq[1])])
        p.take('raw', kr, ('op_hi', kr), ('op_lo', kr))
        p.step('evac', kr, rows=(0, DA), n=NTOK)
        for t, k in enumerate(cq):
            p.step('gn', k, bc=cq[1], n=nq, g=(l, 80 + t))
            p.step('qks', k, src='raw', rows=(0, P), n=nq, dst=('cq', t))
        p.take('acc', ('rot', kr), ('rope_sin', kr))
        p.step('rot', kr, rows=DA, t='A', normed=False)
        p.take('tmp', ('rope', kr), ('roped', kr))
        p.step('rope', kr, rows=DA, t='A')
        p.step('qks', kr, src='raw', rows=(NOPE, DA), n=NTOK, dst=('kr', 0))

        units = [('A', h, [h]) for h in range(8)] + [('B', j, [j, j + 4]) for j in range(4)] \
            + [('C', j, [2 * j, 2 * j + 1]) for j in range(4)] + [('D', j, [j, j + 4]) for j in range(4)]
        kgen, items, of_unit = {}, [], []
        for b, j, heads in units:
            u = (l, b, j)
            kgen[u] = (l, b, 0) if b in 'BD' else u
            mine = []
            for h in heads:
                mine += [(u, h, 'x', 0), (u, h, 'x', 1)] + ([] if last else [(u, h, 'c', 0)])
            items += mine
            of_unit.append(mine)
        last_item = {}
        for it in items:
            last_item[it[0]] = it
            last_item['K', kgen[it[0]]] = it

        def pieces_then(make):
            steps = []

            def first():
                steps.extend(make())
                S.append(steps.pop(0))
            return first, lambda: S.append(steps.pop(0))

        def chain(key, kind, n, make, ring, gen, free, rows=P, g=None):
            first, rest = pieces_then(make)
            out = [first] if kind == 'A' else [first, rest]

            def evac():
                p.take('raw', key, ('op_hi', key), ('op_lo', key))
                p.step('evac', key, rows=(0, rows), n=n)
                if kind == 'D':
                    p.take('fil', key, ('stat_sum', key))
                    p.step('evacsq', key, rows=(0, rows), n=n)

            def stat():
                p.take('acc', ('stat', key), ('stat_mean', key))
                p.step('stat', key, srcs=[key], nh=2, dim=DH, n=n)

            def gain():
                p.take('acc', ('bc', key), ('normed', key))
                p.step('bcast', key, n=n)
                p.step('gn', key, bc=key, n=n, g=g)

            def rotate():
                t = 'A' if kind == 'A' else 'B'
                p.take('acc', ('rot', key), ('rope_sin', key))
                p.step('rot', key, rows=rows, t=t, normed=kind == 'D')
                p.take('tmp', ('rope', key), ('roped', key))
                p.step('rope', key, rows=rows, t=t)

            def store():
                p.take(ring, gen, free)
                p.step('qks', key, src='acc' if kind == 'C' else 'raw', rows=(0, rows), n=n, dst=(ring, gen))
            if kind != 'C':
                out.append(evac)
            if kind == 'D':
                out += [stat, gain]
            if kind != 'C':
                out.append(rotate)
            return out + [store]

        def v_chain(key, gen, free, wide, make=None):
            out = []

            def evac():
                p.take('raw', key, ('v_turned', key))
                p.step('evac', key, rows=(P - wide, P), n=NTOK)

            def turn():
                p.take('acc', ('vtr', key), ('v_lo', key))
                p.step('vtr', key, wide=wide)

            def store():
                p.take('V', gen, free)
                p.step('vs', key, wide=wide, dst=gen)
            if make:
                out += list(pieces_then(make))
            return out + [evac, turn, store]

        def projection(u):
            _, b, j = u
            gen = kgen[u]
            qfree = ('scores', last_item[u])
            kfree = ('scores', last_item['K', gen])
            vfree = ('pv_done', last_item['K', gen][:3])
            if b == 'A':
                key, qkey = (l, 'A', 'kv', j), (l, 'A', 'q', j)

                def kv():
                    S.extend(p.gemm(key, [dict(w='ukv', l=l, h=j)], 'ckv', lambda _: range(1), P, NTOK,
                                    [('op_lo', key), ('raw_ready', key)], {0: [('op_lo', ckv)]}))

                def kstore():
                    p.take('K', gen, kfree)
                    p.step('qks', key, src='acc', rows=(0, NOPE), n=NTOK, dst=('K', gen))
                qs = chain(qkey, 'A', nq, lambda: p.gemm(
                    qkey, [dict(w='uq', l=l, h=j)], 'cq', lambda _: range(2), DA, nq, [('raw_ready', qkey)],
                    {0: [('op_lo', cq[1]), ('op_lo', cq[0])]}), 'Q', u, qfree, rows=DA)
                vs = v_chain(key, gen, vfree, DH)
                return [qs[0], kv, qs[1], vs[0], kstore, qs[2], vs[1], qs[3], vs[2]]
            low = b.lower()
            halves = [j, j + 4] if b in 'BD' else None
            own = j * P if b == 'C' else 0
            done = 'op_lo' if b == 'C' else 'rawsq_ready' if b == 'D' else 'raw_ready'
            qkey, nkey, vkey = ((l, b, x, j) for x in 'qkv')
            qs = chain(qkey, b, nq, lambda: proj(low + '_q', qkey, nq, c0=j * P, halves=halves,
                                                 frees=[(done, qkey)]), 'Q', u, qfree, g=(l, 83))
            if gen != u and j:
                return qs
            ks = chain(nkey, b, NTOK, lambda: proj(low + '_k', nkey, NTOK, c0=own, frees=[(done, nkey)]),
                       'K', gen, kfree, g=(l, 84))
            vs = v_chain(vkey, gen, vfree, P, lambda: proj(low + '_v', vkey, NTOK, c0=own,
                                                           frees=[('raw_ready', vkey)]))
            if b == 'C':
                return ks + qs + vs
            if b == 'B':
                return ks[:3] + qs[:2] + [ks[3], qs[2]] + vs[:3] + [qs[3], ks[4], vs[3], qs[4], vs[4]]
            return ks[:3] + qs[:2] + [ks[3], qs[2], ks[4], vs[0], vs[1], ks[5], vs[2], qs[3], ks[6], qs[4], vs[3], qs[5],
                                      vs[4], qs[6]]

        def bias_steps(u, i):
            if i == 0:
                p.take('bias', u, ('scores', last_item[u]))
            p.take('tab', (u, i), ('bias_full', (u, i)))
            p.step('tab', (u, i))
            p.step('bias', (u, i), l=l)

        def emit(item_no):
            k = item_no
            if 1 <= k <= len(items):
                if items[k - 1][0][1] == 'B':
                    p.step('sinksum', items[k - 1])
                p.step('den', items[k - 1])
            if 2 <= k < len(items) + 2:
                it2 = items[k - 2]
                g = it2[:3]
                if it2[3] == 0:
                    p.take('PT', g, ('pv_done', g))
                p.take('T', it2, ('pt_lo', it2))
                p.step('tr', it2)
                p.step('trs', it2)
            if k < len(items):
                it = items[k]
                p.take('S', it, ('exp_done', it))
                p.take('P', it, ('prob_ready', it))
                p.take('Pn', it, ('p_turned', it))
                p.take('small', it, ('prob_ready', it))
                p.step('sc', it)
                p.step('mx', it)

        def emit_pv(k):
            if 2 <= k < len(items) + 2 and (items[k - 2][2] == 'c' or items[k - 2][3] == 1):
                g = items[k - 2][:3]
                p.take('pv', g, ('o_lo', g))
                p.step('pv', g)
                p.step('ov', g)

        class Merge:

            def __init__(self):
                self.todo = [(n, stage) for n in range(3) for dt in range(KT) for stage in self.stages(dt, n, 'merge')]

            def stages(self, dt, n, ring):
                k = (l, dt, n)
                end = items[(n + 1) * len(items) // 4 - 1][:3]

                def gate():
                    S.extend(p.gemm(('gate', k), [dict(w='w_in', l=l, row=4 * j, nk=4, cols=P,
                                                       starts=[OFF['gate'] + n * D + dt * P]) for j in range(2)],
                                    'U', lambda j: range(4 * j, 4 * j + 4), P, nq, [('gate_tanh', k)], ring=ring))

                def sig():
                    p.take('sig', k, ('gate_mul', k))
                    p.step('gsig', k, n=nq)

                def up():
                    S.extend(p.gemm(('up', k), [dict(w='w_branch', l=l, b=n, row=0, nk=4, cols=P, starts=[dt * P])],
                                    'O', lambda _: range(4 * n, 4 * n + 4), P, nq, [('gate_mul', k)],
                                    {0: [('o_lo', end)]}, ring=ring))

                def mul():
                    if n:
                        p.take('fil', ('gate', k), ('gate_acc', k))
                    p.step('gmul', k, n=nq)
                    if n:
                        p.step('gacc', k, n=nq)
                return [gate, sig, up, mul]

            def left(self, n):
                return self.todo and self.todo[0][0] < n

            def advance(self):
                self.todo.pop(0)[1]()

        merge = Merge()
        per = len(items) // 4

        def merge_some(*which):
            if not merge.todo or merge.todo[0][1].__name__ not in which or slot < (merge.todo[0][0] + 1) * per + 2:
                return
            merge.advance()

        p.kgen.update(kgen)
        for micro in projection((l, 'A', 0)):
            micro()
        at_item = 0
        for un, mine in enumerate(of_unit):
            micro = []
            if un + 1 < len(units):
                u2 = (l, *units[un + 1][:2])
                micro = projection(u2)
            keep = micro.pop() if micro and len(micro) > 7 or micro and units[un + 1][0] == 'A' else None
            put = 0
            for i in range(len(mine)):
                slot = at_item + i
                ex_at = EX_AT[slot // per]
                if l == 0 and slot == 2 * per:
                    mods.rest(0)
                emit(slot)
                merge_some('sig', 'mul')
                if l == 0 and slot < 2 * per:
                    mods.some(MOD_RATE[slot // per])
                upto = -(-len(micro) * (i + 1) // len(mine))
                if len(mine) - i <= 2 and un + 1 < len(units) and units[un + 1][0] == 'C':
                    while merge.left(1):
                        merge.advance()
                    bias_steps(u2, i - len(mine) + 2)
                for m_no, m in enumerate(micro[put:upto]):
                    if m_no == ex_at:
                        p.step('ex', mine[i])
                    m()
                if upto - put <= ex_at:
                    p.step('ex', mine[i])
                put = upto
                emit_pv(at_item + i)
                merge_some('gate', 'up')
                if keep and i == len(mine) - 1:
                    keep()
            at_item += len(mine)
        for i in range(2):
            emit(at_item + i)
            emit_pv(at_item + i)
        while merge.left(3):
            merge.advance()
        for dt in range(KT):
            for stage in merge.stages(dt, 3, 'acc'):
                stage()
            if dt:
                p.step('ms', (l, dt - 1), n=nq)
        p.step('ms', (l, KT - 1), n=nq)

        def output(name, nmo, pieces_of, src, kts, need):
            for dt in range(KT):
                key = (nmo, dt)
                S.extend(p.gemm(('y', key), pieces_of(dt), src, kts, P, nq, [('sq_done', key)],
                                need if dt == 0 else {}))
                if dt:
                    square_sum(nmo, dt - 1, nq)
                p.step('yev', key, n=nq)
                square(nmo, dt, nq, 'Y', ('piece_used', (('y', key), len(p.tile['y', key]['pieces']) - 1)))
            square_sum(nmo, KT - 1, nq)

        nmo = (l, 'post_mix')
        output('w_out', nmo, lambda dt: [dict(w='w_out', l=l, row=4 * j, nk=4, cols=P, starts=[dt * P])
                                         for j in range(2)], 'M', lambda j: range(4 * j, 4 * j + 4),
               {j: [('m_lo', (l, 4 * j + 3))] for j in range(2)})
        norm_stat(nmo, None, 1, D, nq, [('post_scaled', (nmo, KT - 1))])
        nm2 = (l, 'pre_ffn')
        post(nmo, l, 0, nq, nm2)
        norm_stat(nm2, None, 1, D, nq, [('ap_scaled', (nm2, KT - 1))])
        apply(nm2, l, 1, nq)
        if not last:
            mods.enter(1, ('post', 'post_scaled', (nmo, KT - 1)))
        for f in range(FT):
            need = {0: [('ap_lo', (nm2, 3))], 1: [('ap_lo', (nm2, 7))]} if f == 0 else {}
            k = (l, f)
            S.extend(p.gemm(('fa', k), [dict(w='w_ffn_in', l=l, row=4 * j, nk=4, cols=P, starts=[f * P])
                                        for j in range(2)], 'U', lambda j: range(4 * j, 4 * j + 4), P, nq,
                            [('ffn_silu', k)], need))
            p.take('tmp', ('ffn', k), ('ffn_h', k))
            p.step('fsig', k, n=nq)
            mods.some(3)
            S.extend(p.gemm(('fb', k), [dict(w='w_ffn_in', l=l, row=4 * j, nk=4, cols=P, starts=[DFF + f * P])
                                        for j in range(2)], 'U', lambda j: range(4 * j, 4 * j + 4), P, nq,
                            [('ffn_h', k)]))
            p.take('fil', ('ffn', k), ('hid_lo', k))
            p.step('fh', k, n=nq)
            mods.some(3)
        if not last:
            mods.rest(l + 1)
        nmf = (l, 'post_ffn')
        output('w_ffn_out', nmf,
               lambda dt: [dict(w='w_ffn_out', l=l, row=4 * j, nk=min(4, FT - 4 * j), cols=P, starts=[dt * P])
                           for j in range(-(-FT // 4))],
               'hid', lambda j: range(4 * j, min(4 * j + 4, FT)),
               {j: [('hid_lo', (l, min(4 * j + 3, FT - 1)))] for j in range(-(-FT // 4))})
        norm_stat(nmf, None, 1, D, nq, [('post_scaled', (nmf, KT - 1))])
        if not last:
            for g in range(3):
                p.step('coef', (l + 1, g))
        post(nmf, l, 1, nq, (l + 1, 'pre_mix') if not last else None)
    for tt in range(SEQ // P):
        for half in range(2):
            p.take('acc', ('tout', tt, half), ('out_copied', (tt, half)))
            p.step('tout', (tt, half))

    use = [key for kind, key, _ in S if kind == 'mm']
    for key in use:
        if key[0][0] not in ('gate', 'up', 'y', 'fa', 'fb'):
            p.on_pool.add(key)
        p.lo[key] = 'w_lo_pool' if key in p.on_pool else 'w_lo_dve'
        p.take('load', key, (p.lo[key], key))
        p.take('w', key, ('piece_used', key))
    order, done, first = [], 0, 0
    for st in S:
        if st[0] in ('mm', 'mstat'):
            while done < min(len(use), first + AHEAD):
                order.append(('split', use[done], {'raises': (p.lo[use[done]],)}))
                done += 1
            first += st[0] == 'mm'
        order.append(st)
    p.steps = order
    at = {(kind, key): i for i, (kind, key, _) in enumerate(order)}
    mod_keys = [key for kind, key, _ in order if kind == 'modw']
    loads = [(at['split', use[i - L_RING]] if i >= L_RING else -1, 0, 'piece', key) for i, key in enumerate(use)]
    for i, key in enumerate(mod_keys):
        free = at[p.mod_after[key][0], p.mod_after[key][2]] if key in p.mod_after else 0
        if i >= RINGS['mod']:
            free = max(free, at['modw', mod_keys[i - RINGS['mod']]])
        loads.append((free, 1, 'mod', key))
    p.loads = [(what, key) for _, _, what, key in sorted(loads, key=lambda v: v[:2])]
    return p


def build(nc, x, c, ctx, c_ctx, w_mod, b_mod, g_pre_mix, g_post_mix, g_pre_ffn, g_post_ffn, w_in, g_a_q, g_a_kv,
          w_a_uq, w_a_ukv, sink_b, bias_rows, g_d_q, g_d_k, w_branch, w_out, w_ffn_in, w_ffn_out, consts, out):
    plan = build_plan()
    steps, tile = plan.steps, plan.tile
    weights = dict(w_in=w_in, w_mod=w_mod, w_branch=w_branch, w_out=w_out, w_ffn_in=w_ffn_in, w_ffn_out=w_ffn_out)

    count, total = {}, {}
    for kind, key, f in steps:
        for name in SIGNALS[kind] + f.get('raises', ()):
            total[name] = total.get(name, 0) + 1
            count[name, key] = total[name]
    landed, at_slot, mod_landed, mod_at = {}, [0] * L_RING, {}, [0] * RINGS['mod']
    for what, key in plan.loads:
        if what == 'mod':
            k = plan.slot['mod', key]
            mod_at[k] += 16
            mod_landed[key] = (k, mod_at[k])
            continue
        pc = tile[key[0]]['pieces'][key[1]]
        k = plan.slot['load', key]
        at_slot[k] += 16 * (len(pc['starts']) if 'starts' in pc else 1)
        landed[key] = (k, at_slot[k])

    with ExitStack() as es:
        def sb(name, shape, dt=F32):
            return es.enter_context(nc.sbuf_tensor(name, shape, dt))

        sem = {name: es.enter_context(nc.semaphore(name)) for name in total}
        load_sem = [es.enter_context(nc.semaphore(f"load{k}")) for k in range(L_RING)]
        mod_load = [es.enter_context(nc.semaphore(f"mod_load{k}")) for k in range(RINGS['mod'])]
        mod0_load = [es.enter_context(nc.semaphore(f"mod0_load{k}")) for k in range(KT)]
        s_first = es.enter_context(nc.semaphore("s_first"))
        s_c = es.enter_context(nc.semaphore("s_c"))
        s_const = es.enter_context(nc.semaphore("s_const"))
        s_rows = es.enter_context(nc.semaphore("s_rows"))
        s_x = es.enter_context(nc.semaphore("s_x"))
        s_init = es.enter_context(nc.semaphore("s_init"))
        s_tab = [es.enter_context(nc.semaphore(f"s_tab{k}")) for k in range(2)]
        s_out = es.enter_context(nc.semaphore("s_out"))

        H = sb("H", [P, KT, NTOK])
        U = [sb(f"U{a}", [P, KT, NTOK], F32R) for a in ('hi', 'lo')]
        with ExitStack() as start:
            mod0_w = start.enter_context(nc.sbuf_tensor("mod0_w", [P, KT, MOD0], F32))
            mod0_acc = start.enter_context(nc.sbuf_tensor("mod0_acc", [P, 2, MOD0_DVE], F32))
            mod0_product = start.enter_context(nc.sbuf_tensor("mod0_product", [P, 2, MOD0_POOL], F32))
        with ExitStack() as over:
            parts = [over.enter_context(nc.sbuf_tensor(name, shape, F32)) for name, shape in (
                ('under0', [P, 2 * QUARTER]), ('mod_place0', [P, RINGS['mod'], 2, MOD_COLS]),
                ('under1', [P, QUARTER - RINGS['mod'] * 2 * MOD_COLS]), ('merge_sum0', [P, 4, NTOK]),
                ('under2', [P, 2 * QUARTER]), ('mod_place1', [P, 2, MOD_COLS]), ('under3', [P, QUARTER - 2 * MOD_COLS]),
                ('merge_sum1', [P, 4, NTOK]))]
        merge_sum, mod_places = (parts[3], parts[7]), (parts[1], parts[5])
        Z = sb("Z", [P, ARENA], F32R)
        Y = sb("Y", [P, FARENA])
        load_ring = sb("load_ring", [P, L_RING, PIECE])
        w_ring = sb("w_ring", [P, W_RING, 2, PIECE], F32R)
        tmp = sb("tmp", [P, 2, NTOK])
        fil = sb("fil", [P, 2, NTOK])
        sig = sb("sig", [P, RINGS['sig'], NTOK])
        wide = sb("wide", [P, NTOK])
        tab = sb("tab", [P, 2, 384])
        C = sb("C", [P, NKEPT])
        ident_r = sb("ident_r", [P, P], F32R)
        mask_r = sb("mask_r", [P, 512], F32R)
        mod_ring1 = Y[:, P_AT:P_AT + RINGS['mod'] * 2 * MOD_COLS].rearrange("p (r k m) -> p r k m", k=2, m=MOD_COLS)
        flat = tab[:, :, :].rearrange("p a b -> p (a b)")
        rows = flat[:, 0:DEPTH * P].rearrange("p (l c) -> p l c", l=DEPTH)
        crows = flat[0:16, DEPTH * P:(DEPTH + 3) * P].rearrange("p (l c) -> p l c", l=3)
        mod_sums1 = flat[:, 0:2 * MOD_COLS].rearrange("p (s m) -> p s m", s=2)
        par = sb("par", [P, DEPTH, ROWS])
        sc = sb("sc", [P, 2, KT])
        mod = sb("mod", [P, DEPTH, 48, 2])
        coef = sb("coef", [P, DEPTH, 4, KT, 2])
        sink = sb("sink", [P, DEPTH, 8])
        sink8 = sb("sink8", [P, DEPTH, 8])
        stat = sb("stat", [P, 3, 8])
        small = sb("small", [P, 2, 12])
        bank = [es.enter_context(nc.psum_tensor(f"bank{i}", [P, 512], F32)) for i in range(8)]

        def const(name, rows_=P):
            return C[0:rows_, CONST[name][0]:CONST[name][1]]

        ident = const('ident')

        def acc(key):
            return bank[6] if ('merge', key) in plan.slot else bank[plan.slot['acc', key]]

        def s_bank(it):
            return bank[3 + plan.slot['S', it]]

        def t_bank(it):
            return bank[5]

        pv_bank, mod0_bank = bank[7], bank[4]

        def mod_w(key):
            return (mod_ring1 if key[0][0] else mod_places[0])[:, plan.slot['mod', key]]

        def mod_sum(l, side):
            return (mod_sums1 if l else mod_places[1])[:, side, :]

        def mod_bank(key):
            return acc(('mod', key)) if key[0] else pv_bank

        def raw(key):
            at = RAW_AT + plan.slot['raw', key] * NTOK
            return Y[:, at:at + NTOK]

        def macc(key):
            return merge_sum[key[1] // 4][:, key[1] % 4, :]

        def y_tile(kt):
            return Y[:, kt * NTOK:(kt + 1) * NTOK]

        def prob(ring, it):
            at = (P_AT if ring == 'P' else PN_AT) + plan.slot[ring, it] * NTOK
            return Y[:, at:at + NTOK]

        def z(at, n=NTOK):
            return Z[:, at:at + n]

        def o_tile(part, i):
            return z((O_HI, O_LO)[part] + i * NTOK)

        def staged(ring, gen, part):
            at = {'Q': Q_AT, 'K': K_AT, 'V': V_AT}[ring] + (2 * plan.slot[ring, gen] + part) * NTOK
            return z(at)

        def pt(g, part):
            return z(PT_AT + (2 * plan.slot['PT', g] + part) * 1024, 1024).rearrange("p (k q) -> p k q", k=4)

        def bias_r(u, i, part):
            at = BIAS_AT[plan.slot['bias', u]] + (2 * i + part) * 384
            return z(at, 384)

        def operand(src, part, kt, n):
            if src == 'U':
                return U[part][:, kt, 0:n]
            at = {'cq': (CQ_HI, CQ_LO), 'ckv': (CKV_HI, CKV_LO), 'O': (O_HI, O_LO), 'M': (M_HI, M_LO),
                  'hid': (H_HI, H_LO)}[src][part] + (kt % 12 if src == 'O' else kt) * NTOK
            return z(at, n)

        def w_slice(key, part, kt):
            pc = tile[key[0]]['pieces'][key[1]]
            s = w_ring[:, plan.slot['w', key], part, :]
            cols = {'uq': DA, 'ukv': P}.get(pc['w'], pc.get('cols'))
            return s[:, kt * cols:(kt + 1) * cols]

        def piece_size(pc):
            return {'uq': 2 * DA, 'ukv': P}.get(pc['w']) or pc['nk'] * pc['cols']

        def last_piece(key):
            return key, len(tile[key]['pieces']) - 1

        def scale_of(it):
            return (DA if it[0][1] == 'A' else DH) ** -0.5

        def subs(it):
            return [(0, NTOK)] if it[2] == 'x' else [(0, CTX), (CTX, 2 * CTX)]

        def is_ab(l, which):
            return coef[:, l, which]

        def shift(l, which, kt, side):
            return mod[:, l, 24 * which + kt, side:side + 1]

        def split_places(eng, key, f):
            r0, r1 = f['rows']
            n = f['n']
            ring, gen = f['dst']
            if f['src'] == 'acc':
                eng.wait_ge(sem['piece_used'], count['piece_used', last_piece(key)])
                src = acc(key)[r0:r1, 0:n]
            else:
                ready = 'roped' if ('roped', key) in count else 'normed'
                eng.wait_ge(sem[ready], count[ready, key])
                src = raw(key)[r0:r1, 0:n]
            if ring in 'QK':
                for name, k_ in plan.freed[ring, gen]:
                    eng.wait_ge(sem[name], count[name, k_])
                return [(staged(ring, gen, 0)[r0:r1, 0:n], staged(ring, gen, 1)[r0:r1, 0:n], src)]
            if ring == 'kr':
                return [(z(K_AT + 2 * k * NTOK)[r0:r1, :], z(K_AT + (2 * k + 1) * NTOK)[r0:r1, :], src)
                        for k in range(2)]
            return [(operand(ring, 0, gen, n), operand(ring, 1, gen, n), src)]

        def v_places(key, f, part):
            w = f['wide']
            dst = staged('V', f['dst'], part).rearrange("p (t w) -> p t w", t=4)[:, :, 0:w]
            return dst, acc(('vtr', key))[:, 0:4 * w].rearrange("p (t w) -> p t w", t=4)

        def pt_places(it, part):
            if it[2] == 'x':
                q0 = it[3] * P
                return pt(it[:3], part)[:, :, q0:q0 + P], t_bank(it)[:, :].rearrange("p (k q) -> p k q", k=4)
            dst = pt(it[:3], part)[:, 0:2, :].rearrange("p k (t q) -> p k t q", t=2)
            return dst, t_bank(it)[:, :].rearrange("p (t k q) -> p k t q", t=2, k=2)

        def v_column(u, h):
            return {'A': 0, 'B': h // 4 * DH, 'C': h % 2 * DH, 'D': h // 4 * DH}[u[1]]

        def o_places(g):
            u, h, side = g
            i = 'ABCD'.index(u[1]) % 3 * 4 + h // 2
            r0 = h % 2 * DH
            t0 = 0 if side == 'x' else SEQ
            return (o_tile(0, i)[r0:r0 + DH, t0:t0 + SEQ], pv_bank[0:DH, 0:SEQ], o_tile(1, i)[r0:r0 + DH, t0:t0 + SEQ])

        block = es.enter_context(nc.Block())

        @block.sync
        def _(sp):
            sp.dma_start(crows[0:8, 0, :], c.rearrange("b (k p) -> (b k) p", p=P)).then_inc(s_c, 16)
            sp.dma_start(crows[8:16, 0, :], c_ctx.rearrange("(k p) -> k p", p=P)).then_inc(s_c, 16)
            sp.dma_start(C[:, 0:NFIRST], consts[:, 0:NFIRST]).then_inc(s_first, 16)
            sp.dma_start(mod0_w[:, 0, :], w_mod[0, 0:P, 0:MOD0]).then_inc(mod0_load[0], 16)
            sp.dma_start(Y[:, 0:2048].rearrange("p (t d) -> p t d", t=2),
                         x.rearrange("b (t p) d -> p (b t) d", p=P)).then_inc(s_x, 16)
            sp.dma_start(Y[:, 2048:4096].rearrange("p (t d) -> p t d", t=2),
                         ctx.rearrange("b (t p) d -> p (b t) d", p=P)).then_inc(s_x, 16)
            for k in range(1, KT - 2):
                sp.dma_start(mod0_w[:, k, :], w_mod[0, k * P:(k + 1) * P, 0:MOD0]).then_inc(mod0_load[k], 16)
            for l in range(DEPTH):
                sp.dma_start(rows[0:48, l, :], b_mod[l].rearrange("(k p) -> k p", p=P)).then_inc(s_rows, 16)
                for i, g in enumerate((g_pre_mix, g_post_mix, g_pre_ffn, g_post_ffn)):
                    sp.dma_start(rows[48 + 8 * i:56 + 8 * i, l, :],
                                 g[l].rearrange("(k p) -> k p", p=P)).then_inc(s_rows, 16)
                sp.dma_start(rows[80:82, l, :], g_a_q[l].rearrange("(k p) -> k p", p=P)).then_inc(s_rows, 16)
                sp.dma_start(rows[82:83, l, :], g_a_kv[l:l + 1, :]).then_inc(s_rows, 16)
                for i, g in enumerate((g_d_q, g_d_k)):
                    for half in range(2):
                        sp.dma_start(rows[83 + i:84 + i, l, half * DH:(half + 1) * DH],
                                     g[l:l + 1, :]).then_inc(s_rows, 16)
                sp.dma_start(sink[:, l, :], sink_b[l:l + 1, :].to_broadcast([P, 8])).then_inc(s_rows, 16)
            for k in range(KT - 2, KT):
                sp.dma_start(mod0_w[:, k, :], w_mod[0, k * P:(k + 1) * P, 0:MOD0]).then_inc(mod0_load[k], 16)
            sp.dma_start(C[:, NFIRST:], consts[:, NFIRST:NKEPT]).then_inc(s_const, 16)
            sp.dma_start(wide[:, :], consts[:, NKEPT:]).then_inc(s_const, 16)
            for what, key in plan.loads:
                if what == 'mod':
                    (l, ch), j = key
                    for name, k_ in plan.freed['mod', key]:
                        sp.wait_ge(sem[name], count[name, k_])
                    if key in plan.mod_after:
                        _, name, k_ = plan.mod_after[key]
                        sp.wait_ge(sem[name], count[name, k_])
                    sp.dma_start(mod_w(key),
                                 w_mod[l, 2 * j * P:2 * (j + 1) * P, ch * P:ch * P + MOD_COLS]
                                 .rearrange("(k p) m -> p k m", p=P)).then_inc(mod_load[mod_landed[key][0]], 16)
                    continue
                pc = tile[key[0]]['pieces'][key[1]]
                for name, k_ in plan.freed['load', key]:
                    sp.wait_ge(sem[name], count[name, k_])
                dst = load_ring[:, plan.slot['load', key], 0:piece_size(pc)]
                done = load_sem[plan.slot['load', key]]
                l = pc['l']
                if pc['w'] == 'uq':
                    h = pc['h']
                    sp.dma_start(dst.rearrange("p (k m) -> p k m", k=2),
                                 w_a_uq[l, :, h * DA:(h + 1) * DA].rearrange("(k p) m -> p k m", p=P)).then_inc(done, 16)
                elif pc['w'] == 'ukv':
                    h = pc['h']
                    sp.dma_start(dst, w_a_ukv[l, :, h * P:(h + 1) * P]).then_inc(done, 16)
                else:
                    w = weights[pc['w']][l, pc['b']] if 'b' in pc else weights[pc['w']][l]
                    m = pc['cols'] // len(pc['starts'])
                    r0 = pc['row'] * P
                    for i, c0 in enumerate(pc['starts']):
                        sp.dma_start(dst.rearrange("p (k m) -> p k m", k=pc['nk'])[:, :, i * m:(i + 1) * m],
                                     w[r0:r0 + pc['nk'] * P, c0:c0 + m].rearrange("(k p) m -> p k m", p=P))\
                            .then_inc(done, 16)
            for tt in range(SEQ // P):
                sp.wait_ge(sem['out_copied'], count['out_copied', (tt, 1)])
                sp.dma_start(out[0, tt * P:(tt + 1) * P, :], Y[:, tt * D:(tt + 1) * D]).then_inc(s_out, 16)
            sp.wait_ge(s_out, 16 * (SEQ // P))

        n_rows = 16 * DEPTH * 12

        @block.gpsimd
        def _(pool):
            for kind, key, f in steps:
                if kind == 'mod0':
                    pool.wait_ge(mod0_load[key], 16)
                    if key == 0:
                        pool.wait_ge(sem['c_done'], 1)
                    elif key > 1:
                        pool.wait_ge(sem['mod0_pool'], key)
                    w = mod0_w[:, key, 0:MOD0_POOL].unsqueeze(1).to_broadcast([P, 2, MOD0_POOL])
                    to = mod0_product[:, :, :] if key else mod0_acc[:, :, 0:MOD0_POOL]
                    ins = pool.tensor_tensor(to, w, sc[:, :, key].unsqueeze(2).to_broadcast([P, 2, MOD0_POOL]), ALU.mult)
                    if key:
                        ins.then_inc(sem['mod0_mult'], 1)
                        pool.wait_ge(sem['mod0_mult'], key)
                        if key == 1:
                            pool.wait_ge(sem['mod0_pool'], 1)
                        ins = pool.tensor_tensor(mod0_acc[:, :, 0:MOD0_POOL], mod0_acc[:, :, 0:MOD0_POOL], to, ALU.add)
                    ins.then_inc(sem['mod0_pool'], 1)
                elif kind in ('stat', 'mstat'):
                    m = f['n'] // P * f['nh']
                    pool.wait_ge(sem['stat_mean'], count['stat_mean', key])
                    if count['stat_rstd', key] > 1:
                        pool.wait_ge(sem['stat_wide'], count['stat_wide', key] - 1)
                    if count['stat_rstd', key] == 1:
                        pool.wait_ge(s_first, 16)
                    pool.tensor_tensor(stat[:, 1, 0:m], stat[:, 0, 0:m], const('power')[:, 0:m],
                                       ALU.pow).then_inc(sem['stat_rstd'], 1)
                elif kind == 'apA':
                    nm, kt = key
                    k2 = ('ap', nm, kt)
                    pool.wait_ge(sem['ap_scaled'], count['ap_scaled', key])
                    for name, k_ in plan.freed['fil', k2]:
                        pool.wait_ge(sem[name], count[name, k_])
                    pool.wait_ge(sem['coef_ready'], count['coef_ready', (f['l'], 2 * f['which'])])
                    for side in range(f['n'] // SEQ):
                        r = slice(side * SEQ, (side + 1) * SEQ)
                        ins = pool.tensor_scalar(fil[:, plan.slot['fil', k2], r], tmp[:, plan.slot['tmp', k2], r],
                                                 is_ab(f['l'], 2 * f['which'])[:, kt, side:side + 1],
                                                 shift(f['l'], f['which'], kt, side), ALU.mult, ALU.add)
                    ins.then_inc(sem['ap_full'], 1)
                elif kind == 'rope':
                    r = f['rows']
                    pool.wait_ge(sem['rotated'], count['rotated', key])
                    pool.tensor_tensor(raw(key)[0:r, 0:SEQ], raw(key)[0:r, 0:SEQ], const('cos' + f['t'], r),
                                       ALU.mult).then_inc(sem['rope_cos'], 1)
                elif kind == 'bias':
                    u, i = key
                    pool.wait_ge(sem['bias_full'], count['bias_full', key])
                    pool.wait_ge(sem['bias_hi'], count['bias_hi', key])
                    pool.tensor_tensor(bias_r(u, i, 1), Y[:, BT_AT:BT_AT + 384], bias_r(u, i, 0).bitcast(F32),
                                       ALU.subtract).then_inc(sem['bias_lo'], 1)
                elif kind == 'den':
                    pool.wait_ge(sem['rec_ready'], count['rec_ready', key])
                    for name, k_ in plan.freed['Pn', key]:
                        pool.wait_ge(sem[name], count[name, k_])
                    m = len(subs(key))
                    w = NTOK // m
                    pool.tensor_tensor(prob('Pn', key).rearrange("p (m k) -> p m k", m=m),
                                       prob('P', key).rearrange("p (m k) -> p m k", m=m),
                                       small[:, plan.slot['small', key], 10:10 + m].unsqueeze(2).to_broadcast([P, m, w]),
                                       ALU.mult).then_inc(sem['prob_ready'], 1)
                elif kind == 'split' and key in plan.on_pool:
                    sz = piece_size(tile[key[0]]['pieces'][key[1]])
                    slot = plan.slot['w', key]
                    pool.wait_ge(load_sem[landed[key][0]], landed[key][1])
                    pool.wait_ge(sem['w_hi'], count['w_hi', key])
                    for name, k_ in plan.freed['w', key]:
                        pool.wait_ge(sem[name], count[name, k_])
                    pool.tensor_tensor(w_ring[:, slot, 1, 0:sz], load_ring[:, plan.slot['load', key], 0:sz],
                                       w_ring[:, slot, 0, 0:sz].bitcast(F32), ALU.subtract).then_inc(sem['w_lo_pool'], 1)
                elif kind == 'gacc':
                    l, dt, n = key
                    pool.wait_ge(sem['gate_mul'], count['gate_mul', key])
                    if n == 1:
                        pool.wait_ge(sem['gate_mul'], count['gate_mul', (l, dt, 0)])
                    else:
                        pool.wait_ge(sem['gate_acc'], count['gate_acc', (l, dt, n - 1)])
                    a = macc((l, dt))[:, 0:f['n']]
                    pool.tensor_tensor(a, a, fil[:, plan.slot['fil', ('gate', key)], 0:f['n']],
                                       ALU.add).then_inc(sem['gate_acc'], 1)
                elif kind == 'fh':
                    n = f['n']
                    pool.wait_ge(sem['ffn_h'], count['ffn_h', key])
                    pool.wait_ge(sem['hid_hi'], count['hid_hi', key])
                    pool.tensor_tensor(operand('hid', 1, key[1], n), fil[:, plan.slot['fil', ('ffn', key)], 0:n],
                                       operand('hid', 0, key[1], n).bitcast(F32),
                                       ALU.subtract).then_inc(sem['hid_lo'], 1)

        @block.scalar
        def _(act):
            for kind, key, f in steps:
                if kind == 'cin':
                    act.wait_ge(s_c, 32)
                    act.activation(crows[:, 1, :], crows[:, 0, :], ACT.Sigmoid).then_inc(sem['c_sig'], 1)
                elif kind == 'init':
                    act.wait_ge(s_const, 32)
                    act.activation(ident_r[:, :], ident, ACT.Copy).then_inc(s_init, 1)
                    act.activation(mask_r[:, :], wide[:, :], ACT.Copy).then_inc(s_init, 1)
                elif kind == 'xin':
                    act.wait_ge(sem['xin_turned'], count['xin_turned', key])
                    act.activation(H[:, key, :], acc(('xin', key))[:, :], ACT.Copy).then_inc(sem['xin_done'], 1)
                elif kind == 'split':
                    sz = piece_size(tile[key[0]]['pieces'][key[1]])
                    act.wait_ge(load_sem[landed[key][0]], landed[key][1])
                    for name, k_ in plan.freed['w', key]:
                        act.wait_ge(sem[name], count[name, k_])
                    act.activation(w_ring[:, plan.slot['w', key], 0, 0:sz], load_ring[:, plan.slot['load', key], 0:sz],
                                   ACT.Copy).then_inc(sem['w_hi'], 1)
                elif kind == 'sq':
                    nm, kt = key
                    n = f['n']
                    act.wait_ge(sem[f['made'][0]], count[f['made']])
                    for name, k_ in plan.freed['fil', ('sq', nm, kt)]:
                        act.wait_ge(sem[name], count[name, k_])
                    dst = fil[:, plan.slot['fil', ('sq', nm, kt)], 0:n]
                    src = H[:, kt, 0:n] if f['what'] == 'H' else acc(('y', key))[:, 0:n]
                    act.activation(dst, src, ACT.Square).then_inc(sem['sq_done'], 1)
                elif kind == 'yev':
                    act.wait_ge(sem['piece_used'], count['piece_used', last_piece(('y', key))])
                    if key == ((0, 'post_ffn'), 0):
                        act.wait_ge(sem['mod_acc'], count['mod_acc', plan.mods_done[1]])
                    act.activation(y_tile(key[1])[:, 0:f['n']], acc(('y', key))[:, 0:f['n']],
                                   ACT.Copy).then_inc(sem['y_ready'], 1)
                elif kind == 'apA':
                    nm, kt = key
                    k2 = ('ap', nm, kt)
                    act.wait_ge(sem['ap_scaled'], count['ap_scaled', key])
                    act.wait_ge(sem['coef_ready'], count['coef_ready', (f['l'], 2 * f['which'])])
                    for side in range(f['n'] // SEQ):
                        r = slice(side * SEQ, (side + 1) * SEQ)
                        ins = act.activation(U[0][:, kt, r], tmp[:, plan.slot['tmp', k2], r], ACT.Identity,
                                             bias=shift(f['l'], f['which'], kt, side),
                                             scale=is_ab(f['l'], 2 * f['which'])[:, kt, side:side + 1])
                    ins.then_inc(sem['ap_hi'], 1)
                elif kind in ('evac', 'evacsq'):
                    r0, r1 = f['rows']
                    n = f['n']
                    act.wait_ge(sem['piece_used'], count['piece_used', last_piece(key)])
                    src = acc(key)[r0:r1, 0:n]
                    if kind == 'evac':
                        for name, k_ in plan.freed['raw', key]:
                            act.wait_ge(sem[name], count[name, k_])
                        act.activation(raw(key)[r0:r1, 0:n], src, ACT.Copy).then_inc(sem['raw_ready'], 1)
                    else:
                        for name, k_ in plan.freed['fil', key]:
                            act.wait_ge(sem[name], count[name, k_])
                        act.activation(fil[r0:r1, plan.slot['fil', key], 0:n], src,
                                       ACT.Square).then_inc(sem['rawsq_ready'], 1)
                elif kind == 'qks':
                    for d in split_places(act, key, f):
                        ins = act.activation(d[0], d[2], ACT.Copy)
                    ins.then_inc(sem['op_hi'], 1)
                elif kind == 'vs':
                    act.wait_ge(sem['v_turned'], count['v_turned', key])
                    for name, k_ in plan.freed['V', f['dst']]:
                        act.wait_ge(sem[name], count[name, k_])
                    dst, src = v_places(key, f, 0)
                    act.activation(dst, src, ACT.Copy).then_inc(sem['v_hi'], 1)
                elif kind == 'tab':
                    k = plan.slot['tab', key]
                    for name, k_ in plan.freed['tab', key]:
                        act.wait_ge(sem[name], count[name, k_])
                    (l, _, j), i = key
                    act.wait_ge(sem['par_done'], count['par_done', DEPTH - 1])
                    act.dma_start(tab[:, k], bias_rows[l, 2 * j + i]).then_inc(s_tab[k], 16)
                elif kind == 'bias':
                    u, i = key
                    act.wait_ge(sem['bias_full'], count['bias_full', key])
                    for name, k_ in plan.freed['bias', u]:
                        act.wait_ge(sem[name], count[name, k_])
                    act.wait_ge(sem['piece_used'], count['piece_used', (('up', (u[0], KT - 1, 0)), 0)])
                    act.activation(bias_r(u, i, 0), Y[:, BT_AT:BT_AT + 384], ACT.Copy).then_inc(sem['bias_hi'], 1)
                elif kind == 'ex':
                    u, h = key[0], key[1]
                    sm = small[:, plan.slot['small', key]]
                    act.wait_ge(sem['negmax_ready'], count['negmax_ready', key])
                    for name, k_ in plan.freed['P', key]:
                        act.wait_ge(sem[name], count[name, k_])
                    ss = subs(key)
                    if u[1] == 'B':
                        act.activation(sm[:, 6:6 + len(ss)], sm[:, 2:2 + len(ss)], ACT.Exp, bias=sink[:, u[0], h:h + 1])
                    for i, (a, b) in enumerate(ss):
                        ins = act.activation(prob('P', key)[:, a:b], s_bank(key)[:, a:b], ACT.Exp,
                                             bias=sm[:, 2 + i:3 + i], scale=scale_of(key), accum_out=sm[:, 4 + i:5 + i])
                    ins.then_inc(sem['exp_done'], 1)
                elif kind == 'trs':
                    act.wait_ge(sem['p_turned'], count['p_turned', key])
                    for name, k_ in plan.freed['PT', key[:3]]:
                        act.wait_ge(sem[name], count[name, k_])
                    dst, src = pt_places(key, 0)
                    act.activation(dst, src, ACT.Copy).then_inc(sem['pt_hi'], 1)
                elif kind == 'ov':
                    act.wait_ge(sem['pv_done'], count['pv_done', key])
                    if key[0] == (0, 'C', 0):
                        act.wait_ge(sem['mod_acc'], count['mod_acc', plan.mods_done[0]])
                    dst, src, _ = o_places(key)
                    act.activation(dst, src, ACT.Copy).then_inc(sem['o_hi'], 1)
                elif kind == 'gsig':
                    n = f['n']
                    act.wait_ge(sem['piece_used'], count['piece_used', last_piece(('gate', key))])
                    for name, k_ in plan.freed['sig', key]:
                        act.wait_ge(sem[name], count[name, k_])
                    act.activation(sig[:, plan.slot['sig', key], 0:n], acc(('gate', key))[:, 0:n],
                                   ACT.Tanh, scale=0.5).then_inc(sem['gate_tanh'], 1)
                elif kind == 'ms':
                    l, dt = key
                    n = f['n']
                    act.wait_ge(sem['gate_acc'], count['gate_acc', (l, dt, 3)])
                    act.activation(operand('M', 0, dt, n), macc(key)[:, 0:n], ACT.Copy, scale=0.5)\
                        .then_inc(sem['m_hi'], 1)
                elif kind == 'fsig':
                    n = f['n']
                    act.wait_ge(sem['piece_used'], count['piece_used', last_piece(('fa', key))])
                    for name, k_ in plan.freed['tmp', ('ffn', key)]:
                        act.wait_ge(sem[name], count[name, k_])
                    act.activation(tmp[:, plan.slot['tmp', ('ffn', key)], 0:n], acc(('fa', key))[:, 0:n],
                                   ACT.Sigmoid).then_inc(sem['ffn_sig'], 1)
                elif kind == 'fh':
                    n = f['n']
                    act.wait_ge(sem['ffn_h'], count['ffn_h', key])
                    act.activation(operand('hid', 0, key[1], n), fil[:, plan.slot['fil', ('ffn', key)], 0:n],
                                   ACT.Copy).then_inc(sem['hid_hi'], 1)
                elif kind == 'tout':
                    tt, half = key
                    act.wait_ge(sem['out_turned'], count['out_turned', key])
                    at = tt * D + half * 512
                    act.activation(Y[:, at:at + 512], acc(('tout', tt, half))[:, :], ACT.Copy)\
                        .then_inc(sem['out_copied'], 1)

        @block.vector
        def _(dve):
            for kind, key, f in steps:
                if kind == 'cin':
                    dve.wait_ge(sem['c_sig'], count['c_sig', key])
                    dve.tensor_tensor(crows[:, 2, :], crows[:, 0, :], crows[:, 1, :], ALU.mult)\
                        .then_inc(sem['c_silu'], 1)
                    dve.wait_ge(sem['c_turned'], count['c_turned', key])
                    dve.tensor_copy(sc[:, :, :], acc(('cin',))[:, 0:16].rearrange("p (s k) -> p s k", s=2))\
                        .then_inc(sem['c_done'], 1)
                elif kind == 'mod0':
                    dve.wait_ge(mod0_load[key], 16)
                    dve.wait_ge(sem['c_done'], 1)
                    if key:
                        dve.wait_ge(sem['mod0_dve'], key)
                    for side in range(2):
                        w, a = mod0_w[:, key, MOD0_POOL:MOD0_DVE], mod0_acc[:, side, MOD0_POOL:]
                        by = sc[:, side, key:key + 1]
                        if key == 0:
                            ins = dve.tensor_scalar(a, w, by, None, ALU.mult)
                        else:
                            ins = dve.scalar_tensor_tensor(out=a, in0=w, scalar=by, in1=a, op0=ALU.mult, op1=ALU.add)
                    ins.then_inc(sem['mod0_dve'], 1)
                elif kind == 'init':
                    dve.wait_ge(s_rows, n_rows)
                    dve.wait_ge(s_const, 32)
                    dve.tensor_scalar(sink8[:, :, :], sink[:, :, :], float(DH) ** 0.5, None, ALU.mult)\
                        .then_inc(s_init, 1)
                elif kind == 'par':
                    dve.wait_ge(sem['par_turned'], count['par_turned', key])
                    dve.tensor_copy(par[:, key, :], acc(('par', key))[:, 0:ROWS]).then_inc(sem['par_done'], 1)
                elif kind == 'split' and key not in plan.on_pool:
                    sz = piece_size(tile[key[0]]['pieces'][key[1]])
                    slot = plan.slot['w', key]
                    dve.wait_ge(load_sem[landed[key][0]], landed[key][1])
                    dve.wait_ge(sem['w_hi'], count['w_hi', key])
                    for name, k_ in plan.freed['w', key]:
                        dve.wait_ge(sem[name], count[name, k_])
                    dve.tensor_tensor(w_ring[:, slot, 1, 0:sz], load_ring[:, plan.slot['load', key], 0:sz],
                                      w_ring[:, slot, 0, 0:sz].bitcast(F32), ALU.subtract).then_inc(sem['w_lo_dve'], 1)
                elif kind == 'modw':
                    (l, ch), j = key
                    dve.wait_ge(mod_load[mod_landed[key][0]], mod_landed[key][1])
                    if j == 0 and count['mod_acc', key] > 1:
                        dve.wait_ge(sem['mod_sum'], count['mod_sum', key[0]] - 1)
                    for i in range(2):
                        kt = 2 * j + i
                        if kt:
                            dve.wait_ge(sem['mod_first' if i else 'mod_acc'], count['mod_acc', key] - 1 + i)
                        for side in range(f['sides']):
                            w, a = mod_w(key)[:, i, :], mod_sum(l, side)
                            by = sc[:, side, kt:kt + 1]
                            if kt == 0:
                                ins = dve.tensor_scalar(a, w, by, None, ALU.mult)
                            else:
                                ins = dve.scalar_tensor_tensor(out=a, in0=w, scalar=by, in1=a, op0=ALU.mult,
                                                                op1=ALU.add)
                        ins.then_inc(sem['mod_acc' if i else 'mod_first'], 1)
                elif kind == 'modadd':
                    l, _ = key
                    c0, c1, ns = f['first'], f['first'] + f['chunks'], f['sides']
                    if c1 * P == MOD0 and l == 0:
                        dve.wait_ge(sem['mod0_sum'], 1)
                        sums = mod0_bank
                    else:
                        dve.wait_ge(sem['mod_sum'], count['mod_sum', key])
                        sums = mod_bank(key)
                    dve.wait_ge(sem['par_done'], count['par_done', l])
                    dve.tensor_tensor(mod[:, l, c0:c1, 0:ns],
                                      sums[:, 0:2 * (c1 - c0)].rearrange("p (c s) -> p c s", s=2)[:, :, 0:ns],
                                      par[:, l, c0:c1].unsqueeze(2).to_broadcast([P, c1 - c0, ns]),
                                      ALU.add).then_inc(sem['mod_ready'], 1)
                elif kind == 'coef':
                    l, g = key
                    dve.wait_ge(sem['mod_ready'], count['mod_ready', (l, (0 if l == 0 else 14, 22, 46)[g])])
                    ns = 2 if l == 0 or g == 0 else 1

                    def gain(i):
                        return par[:, l, 48 + 8 * i:56 + 8 * i].unsqueeze(2).to_broadcast([P, KT, ns])
                    if g != 1:
                        at = (8, 0, 32)[g]
                        ins = dve.scalar_tensor_tensor(out=coef[:, l, g, :, 0:ns], in0=mod[:, l, at:at + 8, 0:ns], scalar=1.0,
                                                       in1=gain(g), op0=ALU.add, op1=ALU.mult)
                    if g:
                        at = (0, 16, 40)[g]
                        ins = dve.tensor_tensor(coef[:, l, 2 * g - 1, :, 0:ns], mod[:, l, at:at + 8, 0:ns],
                                                gain(2 * g - 1), ALU.mult)
                    ins.then_inc(sem['coef_ready'], 1)
                elif kind in ('stat', 'mstat'):
                    m = f['n'] // P * f['nh']
                    if kind == 'stat':
                        dve.wait_ge(sem['stat_sum'], count['stat_sum', key])
                        sums = acc(('stat', key))
                    else:
                        dve.wait_ge(sem['sq_summed'], count['sq_summed', (key, KT - 1)])
                        sums = pv_bank
                    if count['stat_mean', key] > 1:
                        dve.wait_ge(sem['stat_rstd'], count['stat_rstd', key] - 1)
                    dve.tensor_scalar(stat[:, 0, 0:m], sums[:, 0:m], 1.0 / f['dim'], EPS, ALU.mult,
                                      ALU.add).then_inc(sem['stat_mean'], 1)
                    dve.wait_ge(sem['stat_rstd'], count['stat_rstd', key])
                    if count['rstd_bcast', key] > 1:
                        dve.wait_ge(sem['rstd_bcast'], count['rstd_bcast', key] - 1)
                    w = P // f['nh']
                    dve.tensor_copy(wide[:, 0:f['n']].rearrange("p (m w) -> p m w", w=w),
                                    stat[:, 1, 0:m].unsqueeze(2).to_broadcast([P, m, w])).then_inc(sem['stat_wide'], 1)
                elif kind == 'apA':
                    nm, kt = key
                    k2 = ('ap', nm, kt)
                    n = f['n']
                    dve.wait_ge(sem['rstd_bcast'], count['rstd_bcast', nm])
                    for name, k_ in plan.freed['tmp', k2]:
                        dve.wait_ge(sem[name], count[name, k_])
                    dve.tensor_tensor(tmp[:, plan.slot['tmp', k2], 0:n], H[:, kt, 0:n], acc(('bc', nm))[:, 0:n],
                                      ALU.mult).then_inc(sem['ap_scaled'], 1)
                elif kind == 'apB':
                    nm, kt = key
                    n = f['n']
                    dve.wait_ge(sem['ap_hi'], count['ap_hi', key])
                    dve.wait_ge(sem['ap_full'], count['ap_full', key])
                    dve.tensor_tensor(U[1][:, kt, 0:n], fil[:, plan.slot['fil', ('ap', nm, kt)], 0:n],
                                      U[0][:, kt, 0:n].bitcast(F32), ALU.subtract).then_inc(sem['ap_lo'], 1)
                elif kind == 'post':
                    nm, kt = key
                    n = f['n']
                    k2 = ('post', nm, kt)
                    dve.wait_ge(sem['rstd_bcast'], count['rstd_bcast', nm])
                    dve.wait_ge(sem['y_ready'], count['y_ready', key])
                    for name, k_ in plan.freed['tmp', k2]:
                        dve.wait_ge(sem[name], count[name, k_])
                    dve.tensor_tensor(tmp[:, plan.slot['tmp', k2], 0:n], y_tile(kt)[:, 0:n], acc(('bc', nm))[:, 0:n],
                                      ALU.mult).then_inc(sem['post_scaled'], 1)
                elif kind == 'posth':
                    nm, kt = key
                    dve.wait_ge(sem['post_scaled'], count['post_scaled', key])
                    dve.wait_ge(sem['coef_ready'], count['coef_ready', (f['l'], 1 + f['which'])])
                    for side in range(f['n'] // SEQ):
                        r = slice(side * SEQ, (side + 1) * SEQ)
                        ins = dve.scalar_tensor_tensor(
                            out=H[:, kt, r], in0=tmp[:, plan.slot['tmp', ('post', nm, kt)], r],
                            scalar=coef[:, f['l'], 1 + 2 * f['which'], kt, side:side + 1], in1=H[:, kt, r],
                            op0=ALU.mult, op1=ALU.add)
                    ins.then_inc(sem['h_new'], 1)
                elif kind == 'gn':
                    n = f['n']
                    l, col = f['g']
                    dve.wait_ge(sem['rstd_bcast'], count['rstd_bcast', f['bc']])
                    dve.wait_ge(sem['raw_ready'], count['raw_ready', key])
                    dve.scalar_tensor_tensor(out=raw(key)[:, 0:n], in0=raw(key)[:, 0:n], scalar=par[:, l, col:col + 1],
                                             in1=acc(('bc', f['bc']))[:, 0:n], op0=ALU.mult,
                                             op1=ALU.mult).then_inc(sem['normed'], 1)
                elif kind == 'rope':
                    r = f['rows']
                    t = tmp[0:r, plan.slot['tmp', ('rope', key)], 0:SEQ]
                    dve.wait_ge(sem['rotated'], count['rotated', key])
                    for name, k_ in plan.freed['tmp', ('rope', key)]:
                        dve.wait_ge(sem[name], count[name, k_])
                    dve.tensor_tensor(t, acc(('rot', key))[0:r, 0:SEQ], const('sin' + f['t'], r),
                                      ALU.mult).then_inc(sem['rope_sin'], 1)
                    dve.wait_ge(sem['rope_sin'], count['rope_sin', key])
                    dve.wait_ge(sem['rope_cos'], count['rope_cos', key])
                    dve.tensor_tensor(raw(key)[0:r, 0:SEQ], raw(key)[0:r, 0:SEQ], t, ALU.add)\
                        .then_inc(sem['roped'], 1)
                elif kind == 'qks':
                    places = split_places(dve, key, f)
                    dve.wait_ge(sem['op_hi'], count['op_hi', key])
                    for hi, lo, src in places:
                        ins = dve.tensor_tensor(lo, src, hi.bitcast(F32), ALU.subtract)
                    ins.then_inc(sem['op_lo'], 1)
                elif kind == 'vs':
                    dve.wait_ge(sem['v_hi'], count['v_hi', key])
                    dst, src = v_places(key, f, 1)
                    hi, _ = v_places(key, f, 0)
                    dve.tensor_tensor(dst, src, hi.bitcast(F32), ALU.subtract).then_inc(sem['v_lo'], 1)
                elif kind == 'bias':
                    u, i = key
                    k = plan.slot['tab', key]
                    dve.wait_ge(s_tab[k], 16 * ((count['bias_full', key] + 1) // 2))
                    if count['bias_full', key] > 1:
                        dve.wait_ge(sem['bias_lo'], count['bias_lo', key] - 1)
                    dve.scalar_tensor_tensor(
                        out=Y[:, BT_AT:BT_AT + 384].rearrange("p (j c) -> p j c", j=6),
                        in0=tab[:, k, :].rearrange("p (j c) -> p j c", j=6), scalar=float(DH) ** 0.5,
                        in1=const('maskC').unsqueeze(1).to_broadcast([P, 6, GRID]), op0=ALU.mult,
                        op1=ALU.add).then_inc(sem['bias_full'], 1)
                elif kind == 'mx':
                    u, h = key[0], key[1]
                    sm = small[:, plan.slot['small', key]]
                    ss = subs(key)
                    m = len(ss)
                    dve.wait_ge(sem['scores'], count['scores', key])
                    for name, k_ in plan.freed['small', key]:
                        dve.wait_ge(sem[name], count[name, k_])
                    dve.tensor_reduce(sm[:, 0:m], s_bank(key)[:, :].rearrange("p (m k) -> p m k", m=m), AX_X,
                                      ALU.max).then_inc(sem['max_ready'], 1)
                    dve.wait_ge(sem['max_ready'], count['max_ready', key])
                    if u[1] == 'B':
                        dve.tensor_scalar(sm[:, 2:2 + m], sm[:, 0:m], sink8[:, u[0], h:h + 1], -scale_of(key), ALU.max,
                                          ALU.mult).then_inc(sem['negmax_ready'], 1)
                    else:
                        dve.tensor_scalar(sm[:, 2:2 + m], sm[:, 0:m], -scale_of(key), None,
                                          ALU.mult).then_inc(sem['negmax_ready'], 1)
                elif kind == 'sinksum':
                    sm = small[:, plan.slot['small', key]]
                    m = len(subs(key))
                    dve.wait_ge(sem['exp_done'], count['exp_done', key])
                    dve.tensor_tensor(sm[:, 8:8 + m], sm[:, 4:4 + m], sm[:, 6:6 + m], ALU.add)\
                        .then_inc(sem['sum_ready'], 1)
                elif kind == 'den':
                    sm = small[:, plan.slot['small', key]]
                    m = len(subs(key))
                    dve.wait_ge(sem['exp_done'], count['exp_done', key])
                    at = 4
                    if key[0][1] == 'B':
                        dve.wait_ge(sem['sum_ready'], count['sum_ready', key])
                        at = 8
                    dve.reciprocal(sm[:, 10:10 + m], sm[:, at:at + m]).then_inc(sem['rec_ready'], 1)
                elif kind == 'trs':
                    dve.wait_ge(sem['pt_hi'], count['pt_hi', key])
                    dst, src = pt_places(key, 1)
                    hi, _ = pt_places(key, 0)
                    dve.tensor_tensor(dst, src, hi.bitcast(F32), ALU.subtract).then_inc(sem['pt_lo'], 1)
                elif kind == 'ov':
                    dve.wait_ge(sem['o_hi'], count['o_hi', key])
                    hi, src, lo = o_places(key)
                    dve.tensor_tensor(lo, src, hi.bitcast(F32), ALU.subtract).then_inc(sem['o_lo'], 1)
                elif kind == 'gmul':
                    l, dt, n_ = key
                    n = f['n']
                    dve.wait_ge(sem['gate_tanh'], count['gate_tanh', key])
                    dve.wait_ge(sem['piece_used'], count['piece_used', last_piece(('up', key))])
                    if n_:
                        for name, k_ in plan.freed['fil', ('gate', key)]:
                            dve.wait_ge(sem[name], count[name, k_])
                        dst = fil[:, plan.slot['fil', ('gate', key)], 0:n]
                    else:
                        dst = macc((l, dt))[:, 0:n]
                    dve.scalar_tensor_tensor(out=dst, in0=sig[:, plan.slot['sig', key], 0:n], scalar=1.0,
                                             in1=acc(('up', key))[:, 0:n], op0=ALU.add,
                                             op1=ALU.mult).then_inc(sem['gate_mul'], 1)
                elif kind == 'ms':
                    l, dt = key
                    n = f['n']
                    dve.wait_ge(sem['m_hi'], count['m_hi', key])
                    dve.scalar_tensor_tensor(out=operand('M', 1, dt, n), in0=macc(key)[:, 0:n], scalar=0.5,
                                             in1=operand('M', 0, dt, n).bitcast(F32), op0=ALU.mult,
                                             op1=ALU.subtract).then_inc(sem['m_lo'], 1)
                elif kind == 'fsig':
                    n = f['n']
                    t = tmp[:, plan.slot['tmp', ('ffn', key)], 0:n]
                    dve.wait_ge(sem['ffn_sig'], count['ffn_sig', key])
                    dve.tensor_tensor(t, t, acc(('fa', key))[:, 0:n], ALU.mult).then_inc(sem['ffn_silu'], 1)
                elif kind == 'fh':
                    n = f['n']
                    dve.wait_ge(sem['ffn_silu'], count['ffn_silu', key])
                    dve.wait_ge(sem['piece_used'], count['piece_used', last_piece(('fb', key))])
                    for name, k_ in plan.freed['fil', ('ffn', key)]:
                        dve.wait_ge(sem[name], count[name, k_])
                    dve.tensor_tensor(fil[:, plan.slot['fil', ('ffn', key)], 0:n],
                                      tmp[:, plan.slot['tmp', ('ffn', key)], 0:n], acc(('fb', key))[:, 0:n],
                                      ALU.mult).then_inc(sem['ffn_h'], 1)

        @block.tensor
        def _(pe):
            pe.wait_ge(s_first, 16)

            def three(dst, lhs, rhs, start, stop):
                pe.matmul(dst, lhs[0], rhs[0], start=start, stop=False)
                pe.matmul(dst, lhs[0], rhs[1], start=False, stop=False)
                return pe.matmul(dst, lhs[1], rhs[0], start=False, stop=stop)

            for kind, key, f in steps:
                if kind == 'cin':
                    pe.wait_ge(sem['c_silu'], count['c_silu', key])
                    pe.transpose(acc(('cin',))[:, 0:16], crows[:, 2, :], ident[0:16, 0:16]).then_inc(sem['c_turned'], 1)
                elif kind == 'par':
                    for name, k_ in plan.freed['acc', ('par', key)]:
                        pe.wait_ge(sem[name], count[name, k_])
                    pe.transpose(acc(('par', key))[:, 0:ROWS], rows[0:ROWS, key, :], ident[0:ROWS, 0:ROWS])\
                        .then_inc(sem['par_turned'], 1)
                elif kind == 'xin':
                    if key == 0:
                        pe.wait_ge(s_x, 32)
                    for name, k_ in plan.freed['acc', ('xin', key)]:
                        pe.wait_ge(sem[name], count[name, k_])
                    for tt in range(NTOK // P):
                        at = tt * D + key * P
                        ins = pe.transpose(acc(('xin', key))[:, tt * P:(tt + 1) * P], Y[:, at:at + P], ident)
                    ins.then_inc(sem['xin_turned'], 1)
                elif kind == 'mm':
                    t, j = key
                    g = tile[t]
                    m, n = g['rows'], g['n']
                    if j == 0:
                        for name, k_ in plan.freed[g['ring'], t]:
                            pe.wait_ge(sem[name], count[name, k_])
                    for name, k in (g['need'].get(j, ()) if g['need'] else ()):
                        pe.wait_ge(sem[name], count[name, k])
                    kts = list(g['kt'](j))
                    lastp = j == len(g['pieces']) - 1
                    pe.wait_ge(sem['w_hi'], count['w_hi', key])
                    pe.wait_ge(sem[plan.lo[key]], count[plan.lo[key], key])
                    for i, kt in enumerate(kts):
                        ins = three(acc(t)[0:m, 0:n], [w_slice(key, a, i) for a in range(2)],
                                    [operand(g['src'], a, kt, n) for a in range(2)], j == 0 and i == 0,
                                    lastp and i == len(kts) - 1)
                    ins.then_inc(sem['piece_used'], 1)
                elif kind == 'mod0':
                    pe.wait_ge(mod0_load[key], 16)
                    if key == 0:
                        pe.wait_ge(sem['c_done'], 1)
                    for c0 in range(MOD0_DVE // P, MOD0 // P):
                        ins = pe.matmul(mod0_bank[:, 2 * c0:2 * c0 + 2], mod0_w[:, key, c0 * P:(c0 + 1) * P],
                                        sc[:, :, key], start=key == 0 and c0 == MOD0_DVE // P, stop=key == KT - 1,
                                        skip_group_check=True)
                    ins.then_inc(sem['mod0_pe'], 1)
                elif kind == 'mod0sum':
                    pe.wait_ge(sem['mod0_pool'], KT)
                    pe.wait_ge(sem['mod0_dve'], KT)
                    for c0 in range(MOD0_DVE // P):
                        for side in range(2):
                            ins = pe.matmul(mod0_bank[:, 2 * c0 + side:2 * c0 + side + 1],
                                            mod0_acc[:, side, c0 * P:(c0 + 1) * P], const('ones'), start=True,
                                            stop=True, skip_group_check=True)
                    ins.then_inc(sem['mod0_sum'], 1)
                elif kind == 'modsum':
                    for name, k_ in plan.freed['acc' if key[0] else 'pv', ('mod', key)]:
                        pe.wait_ge(sem[name], count[name, k_])
                    pe.wait_ge(sem['mod_acc'], count['mod_acc', (key, KT // 2 - 1)])
                    for c0 in range(MOD_COLS // P):
                        for side in range(f['sides']):
                            ins = pe.matmul(mod_bank(key)[:, 2 * c0 + side:2 * c0 + side + 1],
                                            mod_sum(key[0], side)[:, c0 * P:(c0 + 1) * P], const('ones'), start=True,
                                            stop=True, skip_group_check=True)
                    ins.then_inc(sem['mod_sum'], 1)
                elif kind == 'init':
                    pe.wait_ge(s_rows, n_rows)
                    pe.wait_ge(s_init, 3)
                elif kind == 'stat':
                    nh = f['nh']
                    for name, k_ in plan.freed['acc', ('stat', key)]:
                        pe.wait_ge(sem[name], count[name, k_])
                    for k in f['srcs']:
                        pe.wait_ge(sem['rawsq_ready'], count['rawsq_ready', k])
                    srcs = [fil[:, plan.slot['fil', k], :] for k in f['srcs']]
                    ones = const('ones') if nh == 1 else const('halves')
                    for tt in range(f['n'] // P):
                        for i, s in enumerate(srcs):
                            ins = pe.matmul(acc(('stat', key))[:, tt * nh:(tt + 1) * nh], s[:, tt * P:(tt + 1) * P], ones,
                                            start=i == 0, stop=i == len(srcs) - 1)
                    ins.then_inc(sem['stat_sum'], 1)
                elif kind == 'sqmm':
                    nm, kt = key
                    if kt == 0 and plan.before[nm]:
                        pe.wait_ge(sem['stat_mean'], count['stat_mean', plan.before[nm]])
                    pe.wait_ge(sem['sq_done'], count['sq_done', key])
                    for tt in range(f['n'] // P):
                        ins = pe.matmul(pv_bank[:, tt:tt + 1], fil[:, plan.slot['fil', ('sq', nm, kt)], tt * P:(tt + 1) * P],
                                        const('ones'), start=kt == 0 and tt == 0, stop=kt == KT - 1,
                                        skip_group_check=True)
                    ins.then_inc(sem['sq_summed'], 1)
                elif kind == 'bcast':
                    for name, k_ in plan.freed['acc', ('bc', key)]:
                        pe.wait_ge(sem[name], count[name, k_])
                    pe.wait_ge(sem['stat_wide'], count['stat_wide', key])
                    for tt in range(f['n'] // P):
                        ins = pe.matmul(acc(('bc', key))[:, tt * P:(tt + 1) * P], wide[:, tt * P:(tt + 1) * P], ident,
                                        start=True, stop=True)
                    ins.then_inc(sem['rstd_bcast'], 1)
                elif kind == 'rot':
                    r = f['rows']
                    for name, k_ in plan.freed['acc', ('rot', key)]:
                        pe.wait_ge(sem[name], count[name, k_])
                    ready = 'normed' if f['normed'] else 'raw_ready'
                    pe.wait_ge(sem[ready], count[ready, key])
                    pe.matmul(acc(('rot', key))[0:r, 0:SEQ], const('rot' + f['t'], r)[:, 0:r], raw(key)[0:r, 0:SEQ],
                              start=True, stop=True).then_inc(sem['rotated'], 1)
                elif kind == 'vtr':
                    w = f['wide']
                    for name, k_ in plan.freed['acc', ('vtr', key)]:
                        pe.wait_ge(sem[name], count[name, k_])
                    pe.wait_ge(sem['raw_ready'], count['raw_ready', key])
                    for tt in range(4):
                        ins = pe.transpose(acc(('vtr', key))[:, tt * w:(tt + 1) * w],
                                           raw(key)[P - w:P, tt * P:(tt + 1) * P], ident[P - w:P, P - w:P])
                    ins.then_inc(sem['v_turned'], 1)
                elif kind == 'sc':
                    u, h, side, qt = key
                    l, b, j = u
                    gen = plan.kgen[u]
                    pe.wait_ge(sem['op_lo'], count['op_lo', (l, b, 'q', j)])
                    pe.wait_ge(sem['op_lo'], count['op_lo', (l, 'A', 'kv', j) if b == 'A' else (l, b, 'k', gen[2])])
                    for name, k_ in plan.freed['S', key]:
                        pe.wait_ge(sem[name], count[name, k_])
                    if b == 'A':
                        pe.wait_ge(sem['op_lo'], count['op_lo', (l, 'kr')])
                        d0, d1 = 0, DA
                    else:
                        d0 = (h // 4 if b in 'BD' else h % 2) * DH
                        d1 = d0 + DH
                    q = [staged('Q', u, a)[d0:d1, :] for a in range(2)]
                    k = [staged('K', gen, a)[d0:d1, :] for a in range(2)]
                    s = s_bank(key)
                    if side == 'x':
                        biased = b in 'BC'
                        ins = three(s[:, :], [x_[:, qt * P:(qt + 1) * P] for x_ in q], k, True, not biased)
                        if b == 'B':
                            ins = pe.matmul(s[:, 0:SEQ], ident_r[:, :], mask_r[:, qt * SEQ:(qt + 1) * SEQ], start=False,
                                            stop=True)
                        if b == 'C':
                            i = h % 2
                            pe.wait_ge(sem['bias_lo'], count['bias_lo', (u, i)])
                            at = (2 - 2 * qt) * GRID
                            pe.matmul(s[:, 0:SEQ], ident_r[:, :], bias_r(u, i, 0)[:, at:at + SEQ], start=False, stop=False)
                            ins = pe.matmul(s[:, 0:SEQ], ident_r[:, :], bias_r(u, i, 1)[:, at:at + SEQ], start=False,
                                            stop=True)
                    else:
                        for t in range(2):
                            ins = three(s[:, t * CTX:(t + 1) * CTX], [x_[:, SEQ + t * P:SEQ + (t + 1) * P] for x_ in q],
                                        [x_[:, SEQ:NTOK] for x_ in k], True, True)
                    ins.then_inc(sem['scores'], 1)
                elif kind == 'tr':
                    for name, k_ in plan.freed['T', key]:
                        pe.wait_ge(sem[name], count[name, k_])
                    pe.wait_ge(sem['prob_ready'], count['prob_ready', key])
                    for i in range(4):
                        ins = pe.transpose(t_bank(key)[:, i * P:(i + 1) * P], prob('Pn', key)[:, i * P:(i + 1) * P], ident)
                    ins.then_inc(sem['p_turned'], 1)
                elif kind == 'pv':
                    u, h, side = key
                    for name, k_ in plan.freed['pv', key]:
                        pe.wait_ge(sem[name], count[name, k_])
                    gen = plan.kgen[u]
                    vkey = (u[0], 'A', 'kv', u[2]) if u[1] == 'A' else (u[0], u[1], 'v', gen[2])
                    pe.wait_ge(sem['v_lo'], count['v_lo', vkey])
                    pe.wait_ge(sem['pt_lo'], count['pt_lo', (u, h, side, 1 if side == 'x' else 0)])
                    c0 = v_column(u, h)
                    v = [staged('V', gen, a).rearrange("p (t w) -> p t w", t=4)[:, :, c0:c0 + DH] for a in range(2)]
                    tiles = range(4) if side == 'x' else range(2, 4)
                    for i, kt in enumerate(tiles):
                        ins = three(pv_bank[0:DH, 0:SEQ], [a[:, kt, :] for a in v],
                                    [pt(key, a)[:, i, :] for a in range(2)], i == 0, i == len(tiles) - 1)
                    ins.then_inc(sem['pv_done'], 1)
                elif kind == 'tout':
                    tt, half = key
                    for name, k_ in plan.freed['acc', ('tout', tt, half)]:
                        pe.wait_ge(sem[name], count[name, k_])
                    for i in range(4):
                        kt = 4 * half + i
                        pe.wait_ge(sem['h_new'], count['h_new', ((DEPTH - 1, 'post_ffn'), kt)])
                        ins = pe.transpose(acc(('tout', tt, half))[:, i * P:(i + 1) * P], H[:, kt, tt * P:(tt + 1) * P],
                                           ident)
                    ins.then_inc(sem['out_turned'], 1)


def constant_table():
    t = np.zeros((P, NCONST), np.float32)

    def put(name, v):
        t[:v.shape[0], CONST[name][0]:CONST[name][0] + v.shape[1]] = v
    tok = np.arange(SEQ)

    def rope(d, rows_):
        half = d // 2
        inv = 10000.0 ** (-np.arange(half // 2, dtype=np.float64) * 2.0 / half)
        cos, sin, rot = np.ones((d, SEQ)), np.zeros((d, SEQ)), np.zeros((d, d))
        for ax, pos in enumerate((tok // GRID, tok % GRID)):
            ang = inv.astype(np.float32)[:, None] * pos.astype(np.float32)[None, :]
            for k in range(2):
                r = slice(ax * half + k * (half // 2), ax * half + (k + 1) * (half // 2))
                cos[r], sin[r] = np.cos(ang), np.sin(ang)
            for i in range(half // 2):
                a, b = ax * half + i, ax * half + half // 2 + i
                rot[b, a], rot[a, b] = -1.0, 1.0
        return cos, sin, rot
    cos, sin, rot = rope(DH, P)
    put('cosB', np.concatenate([cos, cos]))
    put('sinB', np.concatenate([sin, sin]))
    put('rotB', np.kron(np.eye(2), rot))
    cos, sin, rot = rope(ROPE, DA)
    put('cosA', np.concatenate([np.ones((NOPE, SEQ)), cos]))
    put('sinA', np.concatenate([np.zeros((NOPE, SEQ)), sin]))
    r = np.zeros((DA, DA))
    r[NOPE:, NOPE:] = rot
    put('rotA', r)
    put('ident', np.eye(P))
    q = np.arange(SEQ)
    m = np.where(np.abs(q[:, None] - q[None, :]) <= 128, 0.0, NEG)
    put('maskB', np.concatenate([m[0:P], m[P:]], axis=1))
    qc = np.arange(P) % GRID
    c0 = np.clip(qc - KWIN // 2, 0, GRID - KWIN)
    kc = np.arange(GRID)
    put('maskC', np.where((kc[None] >= c0[:, None]) & (kc[None] < c0[:, None] + KWIN), 0.0, NEG))
    put('halves', np.kron(np.eye(2), np.ones((DH, 1))))
    put('ones', np.ones((P, 1)))
    put('power', np.full((P, 8), -0.5))
    return t


def bias_layout(rpb):
    a = np.arange(P)[:, None, None] // GRID
    qc = np.arange(P)[:, None, None] % GRID
    j = np.arange(6)[None, :, None]
    kc = np.arange(GRID)[None, None, :]
    dr = j - 2 - a + 7 + 0 * kc
    dc = np.clip(kc - qc, -(KWIN - 1), KWIN - 1) + (KWIN - 1) + 0 * j
    return np.ascontiguousarray(rpb[:, :, dr, dc].reshape(rpb.shape[0], rpb.shape[1], P, 6 * GRID))


_INS = ['x', 'c', 'ctx', 'c_ctx', 'w_mod', 'b_mod', 'g_pre_mix', 'g_post_mix', 'g_pre_ffn', 'g_post_ffn', 'w_in',
        'g_a_q', 'g_a_kv', 'w_a_uq', 'w_a_ukv', 'sink_b', 'rpb_c', 'g_d_q', 'g_d_k', 'w_branch', 'w_out', 'w_ffn_in',
        'w_ffn_out']


def kernel(**inputs):
    import concourse.bacc as bacc
    from concourse.bass_utils import run_bass_kernel_spmd as run

    nc = bacc.Bacc("TRN2", target_bir_lowering=False, num_devices=1, dynamic_dma_scratch_size=512)
    arrays, args = {}, []
    for name in _INS:
        a = np.asarray(inputs[name])
        a = bias_layout(a) if name == 'rpb_c' else np.ascontiguousarray(a)
        arrays[f"in_{name}"] = a
        args.append(nc.dram_tensor(f"in_{name}", a.shape, mybir.dt.from_np(a.dtype), kind="ExternalInput").ap())
    arrays["in_consts"] = constant_table()
    args.append(nc.dram_tensor("in_consts", (P, NCONST), F32, kind="ExternalInput").ap())
    out = nc.dram_tensor("out_0", (1, SEQ, D), F32, kind="ExternalOutput").ap()
    build(nc, *args, out)
    r = run(nc, [arrays], core_ids=[0])
    return r.results[0]["out_0"]
```
